# Optimizing a Trainium2 kernel written in Bass

```python
import math
import jax, jax.numpy as jnp
from jax import lax
import numpy as np

D_MODEL = 2048
BATCH = 1
SEQ = 256
DEPTH = 1

MIX_WIDTH = D_MODEL
ATTN_WIDTH = MIX_WIDTH // 2
CONV_WIDTH = MIX_WIDTH - ATTN_WIDTH
N_HEADS = 8
HEAD_DIM = ATTN_WIDTH // N_HEADS
QK_DIM = HEAD_DIM // 2
CONV_K = 3
D_FF = ((8 * D_MODEL + 3 * 256 - 1) // (3 * 256)) * 256
N_BUCKETS = 32
MAX_DISTANCE = 128
Q_BLOCK = 128
NORM_EPS = 1e-6
SUBLN_EPS = 1e-5
IN_COLS = 3 * ATTN_WIDTH + 3 * CONV_WIDTH


def rms_norm(x, g, eps=NORM_EPS):
    xf = x.astype(jnp.float32)
    y = xf * lax.rsqrt(jnp.mean(xf * xf, axis=-1, keepdims=True) + eps)
    return (y * g.astype(jnp.float32)).astype(x.dtype)

def rel_bucket(dist):
    n = jnp.maximum(dist, 0)
    max_exact = N_BUCKETS // 2
    nf = jnp.maximum(n, max_exact).astype(jnp.float32)
    large = max_exact + (jnp.log(nf / max_exact) / math.log(MAX_DISTANCE / max_exact)
                         * (N_BUCKETS - max_exact)).astype(jnp.int32)
    large = jnp.minimum(large, N_BUCKETS - 1)
    return jnp.where(n < max_exact, n, large)

def diff_attention(q, k, v, lam, rel_bias):
    b, s = q.shape[0], q.shape[1]
    nb = s // Q_BLOCK
    scale = QK_DIM ** -0.5
    k_pos = jnp.arange(s, dtype=jnp.int32)
    q_blocks = q.reshape(b, nb, Q_BLOCK, N_HEADS, 2, QK_DIM).transpose(1, 0, 2, 3, 4, 5)
    starts = jnp.arange(nb, dtype=jnp.int32) * Q_BLOCK

    def block(args):
        q_blk, start = args
        q_pos = start + jnp.arange(Q_BLOCK, dtype=jnp.int32)
        dist = q_pos[:, None] - k_pos[None, :]
        bias = jnp.transpose(rel_bias[rel_bucket(dist)], (2, 0, 1)).astype(jnp.float32)
        logits = jnp.einsum('bqhcd,bkhcd->bhcqk', q_blk, k).astype(jnp.float32) * scale
        logits = logits + bias[None, :, None]
        logits = jnp.where(dist >= 0, logits, -jnp.inf)
        p = jax.nn.softmax(logits, axis=-1)
        w = (p[:, :, 0] - lam * p[:, :, 1]).astype(v.dtype)
        return jnp.einsum('bhqk,bkhe->bqhe', w, v)

    o = lax.map(block, (q_blocks, starts))
    return o.transpose(1, 0, 2, 3, 4).reshape(b, s, N_HEADS, HEAD_DIM)

def short_conv(h, w):
    return lax.conv_general_dilated(
        h, w[:, None, :].astype(h.dtype), window_strides=(1,),
        padding=[(CONV_K - 1, 0)], dimension_numbers=('NWC', 'WIO', 'NWC'),
        feature_group_count=h.shape[-1])

def first_inputs(seed: int = 0) -> dict:
    key = jax.random.key(seed)
    ks = jax.random.split(key, 20)
    f32 = jnp.float32
    nrm = lambda k, shape, s: jax.random.normal(k, shape, f32) * s
    gain = lambda k, shape: 1.0 + 0.05 * jax.random.normal(k, shape, f32)
    return {
        "x": jax.random.normal(ks[0], (BATCH, SEQ, D_MODEL), f32),
        "w_in": nrm(ks[1], (DEPTH, D_MODEL, IN_COLS), D_MODEL ** -0.5),
        "w_out": nrm(ks[2], (DEPTH, MIX_WIDTH, D_MODEL), MIX_WIDTH ** -0.5),
        "lambda_q1": nrm(ks[3], (DEPTH, QK_DIM), 0.1),
        "lambda_k1": nrm(ks[4], (DEPTH, QK_DIM), 0.1),
        "lambda_q2": nrm(ks[5], (DEPTH, QK_DIM), 0.1),
        "lambda_k2": nrm(ks[6], (DEPTH, QK_DIM), 0.1),
        "subln_gain": gain(ks[7], (DEPTH, HEAD_DIM)),
        "conv_w": nrm(ks[8], (DEPTH, CONV_K, CONV_WIDTH), CONV_K ** -0.5),
        "conv_norm_gain": gain(ks[9], (DEPTH, CONV_WIDTH)),
        "rel_bias": nrm(ks[10], (N_BUCKETS, N_HEADS), 0.5),
        "w_gate": nrm(ks[11], (DEPTH, D_MODEL, D_FF), D_MODEL ** -0.5),
        "w_up": nrm(ks[12], (DEPTH, D_MODEL, D_FF), D_MODEL ** -0.5),
        "w_down": nrm(ks[13], (DEPTH, D_FF, D_MODEL), D_FF ** -0.5),
        "norm_mix_pre": gain(ks[14], (DEPTH, D_MODEL)),
        "norm_mix_post": gain(ks[15], (DEPTH, D_MODEL)),
        "norm_ffn_pre": gain(ks[16], (DEPTH, D_MODEL)),
        "norm_ffn_post": gain(ks[17], (DEPTH, D_MODEL)),
    }

def first_block(x, w_in, w_out, lambda_q1, lambda_k1, lambda_q2, lambda_k2, subln_gain,
              conv_w, conv_norm_gain, rel_bias, w_gate, w_up, w_down,
              norm_mix_pre, norm_mix_post, norm_ffn_pre, norm_ffn_post):
    b, s, _ = x.shape
    A, C = ATTN_WIDTH, CONV_WIDTH
    split_at = [A, 2 * A, 3 * A, 3 * A + C, 3 * A + 2 * C]
    for l in range(DEPTH):
        lambda_init = 0.8 - 0.6 * math.exp(-0.3 * l)
        hn = rms_norm(x, norm_mix_pre[l])
        proj = hn @ w_in[l]
        q, k, v, gate_b, gate_c, hc = jnp.split(proj, split_at, axis=-1)
        q = q.reshape(b, s, N_HEADS, 2, QK_DIM)
        k = k.reshape(b, s, N_HEADS, 2, QK_DIM)
        v = v.reshape(b, s, N_HEADS, HEAD_DIM)
        lam = (jnp.exp(jnp.sum(lambda_q1[l].astype(jnp.float32) * lambda_k1[l].astype(jnp.float32)))
               - jnp.exp(jnp.sum(lambda_q2[l].astype(jnp.float32) * lambda_k2[l].astype(jnp.float32)))
               + lambda_init)
        a = diff_attention(q, k, v, lam, rel_bias)
        a = rms_norm(a, subln_gain[l], SUBLN_EPS) * (1.0 - lambda_init)
        a = a.reshape(b, s, A)
        c = gate_b * short_conv(gate_c * hc, conv_w[l])
        c = rms_norm(c, conv_norm_gain[l])
        mix = jnp.concatenate([a, c], axis=-1) @ w_out[l]
        x = x + rms_norm(mix, norm_mix_post[l])
        hn = rms_norm(x, norm_ffn_pre[l])
        f = (jax.nn.silu(hn @ w_gate[l]) * (hn @ w_up[l])) @ w_down[l]
        x = x + rms_norm(f, norm_ffn_post[l])
    return x


N_META = 16
HEAD_DIM_2 = 64
RWKV_HEADS = 16
RWKV_WIDTH = RWKV_HEADS * HEAD_DIM_2
FOX_HEADS = 16
FOX_WIDTH = FOX_HEADS * HEAD_DIM_2
DECAY_LORA = 96
AAA_LORA = 96
GATE_LORA = 256
D_FF_2 = -(-8 * D_MODEL // (3 * 256)) * 256
RMS_EPS = 1e-6
GN_EPS = 64e-5
ATTN_SCALE = HEAD_DIM_2 ** -0.5

RWKV_SPLITS = (RWKV_WIDTH, 2 * RWKV_WIDTH, 3 * RWKV_WIDTH,
               3 * RWKV_WIDTH + DECAY_LORA, 3 * RWKV_WIDTH + DECAY_LORA + AAA_LORA)
RWKV_COLS = 3 * RWKV_WIDTH + DECAY_LORA + AAA_LORA + GATE_LORA
FOX_SPLITS = (FOX_WIDTH, 2 * FOX_WIDTH, 3 * FOX_WIDTH)
FOX_COLS = 3 * FOX_WIDTH + FOX_HEADS
N_IN = RWKV_COLS + FOX_COLS + 2 * D_MODEL


F32 = jnp.float32

def _rms(x, g):
    xf = x.astype(F32)
    xf = xf * lax.rsqrt(jnp.mean(xf * xf, axis=-1, keepdims=True) + RMS_EPS)
    return xf.astype(x.dtype) * g

def _wkv7_scan(r, w, k, v, a, b):
    B, L, H, N = r.shape

    def step(S, inp):
        r_t, w_t, k_t, v_t, a_t, b_t = inp
        sa = jnp.einsum('bhvk,bhk->bhv', S, a_t)
        S = (S * w_t[:, :, None, :] + sa[..., None] * b_t[:, :, None, :]
             + v_t[..., None] * k_t[:, :, None, :])
        return S, jnp.einsum('bhvk,bhk->bhv', S, r_t)

    xs = tuple(jnp.swapaxes(t, 0, 1) for t in (r, w, k, v, a, b))
    _, y = lax.scan(step, jnp.zeros((B, H, N, N), F32), xs)
    return jnp.swapaxes(y, 0, 1)

def _rwkv7(z, w0, w2, a0, a2, g2, k_k, k_a, r_k, gn_w, gn_b):
    B, L, _ = z.shape
    r, k, v, wd, ad, gd = jnp.split(z, RWKV_SPLITS, axis=-1)
    w_log = -jax.nn.softplus(-(w0 + jnp.tanh(wd) @ w2).astype(F32)) - 0.5
    decay = jnp.exp(-jnp.exp(w_log))
    a = jax.nn.sigmoid((a0 + ad @ a2).astype(F32))
    g = jax.nn.sigmoid(gd) @ g2
    heads = lambda t: t.reshape(B, L, RWKV_HEADS, HEAD_DIM_2)
    kk = heads((k * k_k).astype(F32))
    kk = kk / jnp.maximum(jnp.sqrt(jnp.sum(kk * kk, axis=-1, keepdims=True)), 1e-12)
    kf = k.astype(F32) * (1.0 + (a - 1.0) * k_a.astype(F32))
    rh, kh, vh, ah, dh = heads(r.astype(F32)), heads(kf), heads(v.astype(F32)), heads(a), heads(decay)
    y = _wkv7_scan(rh, dh, kh, vh, -kk, kk * ah)
    mu = jnp.mean(y, axis=-1, keepdims=True)
    var = jnp.mean(jnp.square(y - mu), axis=-1, keepdims=True)
    y = (y - mu) * lax.rsqrt(var + GN_EPS)
    y = y * gn_w.astype(F32).reshape(RWKV_HEADS, HEAD_DIM_2) + gn_b.astype(F32).reshape(RWKV_HEADS, HEAD_DIM_2)
    y = y + jnp.sum(rh * kh * r_k.astype(F32), axis=-1, keepdims=True) * vh
    return y.reshape(B, L, RWKV_WIDTH).astype(z.dtype) * g

def _fox(z, q_g, k_g, f_bias):
    B, L, _ = z.shape
    q, k, v, fl = jnp.split(z, FOX_SPLITS, axis=-1)
    q = _rms(q.reshape(B, L, FOX_HEADS, HEAD_DIM_2), q_g)
    k = _rms(k.reshape(B, L, FOX_HEADS, HEAD_DIM_2), k_g)
    v = v.reshape(B, L, FOX_HEADS, HEAD_DIM_2)
    log_f = jax.nn.log_sigmoid(fl.astype(F32) + f_bias.astype(F32))
    c = jnp.swapaxes(jnp.cumsum(log_f, axis=1), 1, 2)
    bounds = [(0, N_META)] + [(s, min(s + Q_BLOCK, L)) for s in range(N_META, L, Q_BLOCK)]
    outs = []
    for s, e in bounds:
        sc = jnp.einsum('bqhd,bkhd->bhqk', q[:, s:e], k[:, :e]).astype(F32) * ATTN_SCALE
        sc = sc + c[:, :, s:e, None] - c[:, :, None, :e]
        causal = jnp.arange(s, e)[:, None] >= jnp.arange(e)[None, :]
        p = jax.nn.softmax(jnp.where(causal, sc, -jnp.inf), axis=-1)
        outs.append(jnp.einsum('bhqk,bkhd->bqhd', p.astype(v.dtype), v[:, :e]))
    return jnp.concatenate(outs, axis=1).reshape(B, L, FOX_WIDTH)

def _layer(h, n1, w_in, mu, w0, w2, a0, a2, g2, k_k, k_a, r_k, gn_w, gn_b,
           q_g, k_g, f_bias, w_a, w_b, w_o, n2, w_gu, w_dn):
    xn = _rms(h, n1)
    proj = xn @ w_in
    z_rwkv, z_fox, z_gate = jnp.split(proj, (RWKV_COLS, RWKV_COLS + FOX_COLS), axis=-1)
    z_prev = jnp.pad(z_rwkv, ((0, 0), (1, 0), (0, 0)))[:, :-1]
    z_rwkv = z_rwkv + (z_prev - z_rwkv) * mu
    y_a = _rwkv7(z_rwkv, w0, w2, a0, a2, g2, k_k, k_a, r_k, gn_w, gn_b)
    y_b = _fox(z_fox, q_g, k_g, f_bias)
    gates = jax.nn.sigmoid(z_gate.astype(F32)).astype(h.dtype)
    g_a, g_b = jnp.split(gates, 2, axis=-1)
    merged = g_a * (y_a @ w_a) + g_b * (y_b @ w_b)
    h = h + merged @ w_o
    gate, up = jnp.split(_rms(h, n2) @ w_gu, 2, axis=-1)
    return h + (jax.nn.silu(gate) * up) @ w_dn

def second_inputs(seed: int = 0) -> dict:
    key = jax.random.key(seed)
    ks = jax.random.split(key, 24)
    nrm = lambda k, shape, scale: jax.random.normal(k, shape, F32) * scale
    Dp = DEPTH
    return {
        'x': nrm(ks[0], (BATCH, SEQ, D_MODEL), 1.0),
        'meta_tokens': nrm(ks[1], (N_META, D_MODEL), 1.0),
        'norm1_g': 1.0 + nrm(ks[2], (Dp, D_MODEL), 0.05),
        'w_in': nrm(ks[3], (Dp, D_MODEL, N_IN), D_MODEL ** -0.5),
        'rwkv_mu': jax.random.uniform(ks[4], (Dp, RWKV_COLS), F32, 0.0, 1.0),
        'rwkv_w0': jax.random.uniform(ks[5], (Dp, RWKV_WIDTH), F32, -5.0, -1.0),
        'rwkv_w2': nrm(ks[6], (Dp, DECAY_LORA, RWKV_WIDTH), 0.5 * DECAY_LORA ** -0.5),
        'rwkv_a0': nrm(ks[7], (Dp, RWKV_WIDTH), 0.1),
        'rwkv_a2': nrm(ks[8], (Dp, AAA_LORA, RWKV_WIDTH), 0.5 * AAA_LORA ** -0.5),
        'rwkv_g2': nrm(ks[9], (Dp, GATE_LORA, RWKV_WIDTH), GATE_LORA ** -0.5),
        'rwkv_k_k': 0.85 + nrm(ks[10], (Dp, RWKV_WIDTH), 0.05),
        'rwkv_k_a': 1.0 + nrm(ks[11], (Dp, RWKV_WIDTH), 0.05),
        'rwkv_r_k': nrm(ks[12], (Dp, RWKV_HEADS, HEAD_DIM_2), 0.1),
        'rwkv_gn_w': 1.0 + nrm(ks[13], (Dp, RWKV_WIDTH), 0.05),
        'rwkv_gn_b': nrm(ks[14], (Dp, RWKV_WIDTH), 0.01),
        'fox_q_norm_g': 1.0 + nrm(ks[15], (Dp, HEAD_DIM_2), 0.05),
        'fox_k_norm_g': 1.0 + nrm(ks[16], (Dp, HEAD_DIM_2), 0.05),
        'fox_f_bias': jax.random.uniform(ks[17], (Dp, FOX_HEADS), F32, 1.0, 4.0),
        'w_branch_a': nrm(ks[18], (Dp, RWKV_WIDTH, D_MODEL), RWKV_WIDTH ** -0.5),
        'w_branch_b': nrm(ks[19], (Dp, FOX_WIDTH, D_MODEL), FOX_WIDTH ** -0.5),
        'w_o': nrm(ks[20], (Dp, D_MODEL, D_MODEL), D_MODEL ** -0.5),
        'norm2_g': 1.0 + nrm(ks[21], (Dp, D_MODEL), 0.05),
        'w_gate_up': nrm(ks[22], (Dp, D_MODEL, 2 * D_FF_2), D_MODEL ** -0.5),
        'w_down': nrm(ks[23], (Dp, D_FF_2, D_MODEL), D_FF_2 ** -0.5),
    }

def second_block(x, meta_tokens, norm1_g, w_in, rwkv_mu, rwkv_w0, rwkv_w2, rwkv_a0, rwkv_a2,
              rwkv_g2, rwkv_k_k, rwkv_k_a, rwkv_r_k, rwkv_gn_w, rwkv_gn_b, fox_q_norm_g,
              fox_k_norm_g, fox_f_bias, w_branch_a, w_branch_b, w_o, norm2_g, w_gate_up, w_down):
    B = x.shape[0]
    meta = jnp.broadcast_to(meta_tokens.astype(x.dtype)[None], (B, N_META, D_MODEL))
    h = jnp.concatenate([meta, x], axis=1)
    for l in range(DEPTH):
        h = _layer(h, norm1_g[l], w_in[l], rwkv_mu[l], rwkv_w0[l], rwkv_w2[l], rwkv_a0[l],
                   rwkv_a2[l], rwkv_g2[l], rwkv_k_k[l], rwkv_k_a[l], rwkv_r_k[l], rwkv_gn_w[l],
                   rwkv_gn_b[l], fox_q_norm_g[l], fox_k_norm_g[l], fox_f_bias[l], w_branch_a[l],
                   w_branch_b[l], w_o[l], norm2_g[l], w_gate_up[l], w_down[l])
    return h[:, N_META:]


def setup_inputs(seed=0):
    out = dict(first_inputs(seed))
    for name, value in second_inputs(seed + 1).items():
        if name != "x":
            out[name + "_2"] = value
    return out


def reference(
    x, w_in, w_out, lambda_q1, lambda_k1, lambda_q2, lambda_k2, subln_gain, conv_w,
    conv_norm_gain, rel_bias, w_gate, w_up, w_down, norm_mix_pre, norm_mix_post, norm_ffn_pre,
    norm_ffn_post, meta_tokens_2, norm1_g_2, w_in_2, rwkv_mu_2, rwkv_w0_2, rwkv_w2_2, rwkv_a0_2,
    rwkv_a2_2, rwkv_g2_2, rwkv_k_k_2, rwkv_k_a_2, rwkv_r_k_2, rwkv_gn_w_2, rwkv_gn_b_2,
    fox_q_norm_g_2, fox_k_norm_g_2, fox_f_bias_2, w_branch_a_2, w_branch_b_2, w_o_2, norm2_g_2,
    w_gate_up_2, w_down_2,
):
    x = first_block(
        x, w_in, w_out, lambda_q1, lambda_k1, lambda_q2, lambda_k2, subln_gain, conv_w,
        conv_norm_gain, rel_bias, w_gate, w_up, w_down, norm_mix_pre, norm_mix_post,
        norm_ffn_pre, norm_ffn_post,
    )
    return second_block(
        x, meta_tokens_2, norm1_g_2, w_in_2, rwkv_mu_2, rwkv_w0_2, rwkv_w2_2, rwkv_a0_2,
        rwkv_a2_2, rwkv_g2_2, rwkv_k_k_2, rwkv_k_a_2, rwkv_r_k_2, rwkv_gn_w_2, rwkv_gn_b_2,
        fox_q_norm_g_2, fox_k_norm_g_2, fox_f_bias_2, w_branch_a_2, w_branch_b_2, w_o_2,
        norm2_g_2, w_gate_up_2, w_down_2,
    )


_drawn_inputs = setup_inputs


def setup_inputs(seed=0):
    import zlib

    import numpy as np

    out = dict(_drawn_inputs(seed))
    spreads = {}
    factors = {'lambda_q1': 3.548,
     'lambda_q2': 56.63,
     'norm1_g_2': 2.999,
     'rwkv_w2_2': 8.0,
     'rwkv_a0_2': 7.363,
     'rwkv_k_k_2': 64.0,
     'rwkv_k_a_2': 5.288,
     'rwkv_gn_w_2': 30.381,
     'rwkv_gn_b_2': 64.0,
     'fox_q_norm_g_2': 8.0,
     'fox_k_norm_g_2': 8.0,
     'norm2_g_2': 8.0}
    for name, (base, spread) in spreads.items():
        noise = np.random.default_rng([zlib.crc32(name.encode()), seed]).standard_normal(out[name].shape)
        drawn = base * np.exp(spread * noise) if base else spread * noise
        out[name] = __import__('jax').numpy.asarray(drawn.astype(out[name].dtype))
    for name, factor in factors.items():
        out[name] = (out[name] * factor).astype(out[name].dtype)
    return out
```

```python
import math
from contextlib import ExitStack

import numpy as np

import concourse.bass as bass
from concourse import mybir

P = 128
D = 2048
SEQ = 256
META = 16
TOK = META + SEQ
KT = D // P
FF = 5632
FT = FF // P
HEADS = 8
HD = 128
QK = 64
CONV_K = 3
BUCKETS = 32
MAX_DIST = 128
CT = 1024 // P
LANES = 16
RHD = 64
LORA = 96
RWKV_COLS = 3 * 1024 + 2 * LORA + 256
FOX0 = RWKV_COLS
GATE0 = RWKV_COLS + 3 * 1024 + LANES
UNIT_K = 4
UNIT_C = 512
RAW = 4
LAMBDA_INIT = 0.2
ARENA = 19400
MASKED = -1e30
DECAY_SCALE = -math.exp(-0.5)
RMS_EPS = 1e-6
SUBLN_EPS = 1e-5
GN_EPS = 64e-5

F32 = mybir.dt.float32
F32R = mybir.dt.float32r
ALU = mybir.AluOpType
ACT = mybir.ActivationFunctionType
AX = mybir.AxisListType.X


def constants():
    p = np.arange(P)
    parts = {}
    parts["ident"] = np.eye(P)
    half = (p[:, None] // RHD) == (p[None, :] // RHD)
    parts["head_sum"] = half.astype(float)
    parts["head_center"] = np.eye(P) - half / RHD
    s, t = p[:, None], p[None, :]
    parts["gram_mask"] = np.concatenate([s < t, s <= t], axis=1)
    parts["upper8"] = (s < t) & (s // 8 == t // 8)
    parts["lower8"] = (s > t) & (s // 8 == t // 8)
    for m in (16, 32, 64, 128):
        parts[f"join{m}"] = (s // m == t // m) & (s % m < m // 2) & (t % m >= m // 2)

    def sums(n):
        s, t = np.arange(n)[:, None], np.arange(n)[None, :]
        mid = (s <= n // 2 - 1).astype(float)
        incl, excl = (s <= t) - mid, (s < t) - mid
        aux = np.concatenate([mid, 1 - mid, np.ones((n, 1))], axis=1)
        m = np.concatenate([incl, excl, aux], axis=1) * DECAY_SCALE
        return np.concatenate([m, np.zeros((P - n, m.shape[1]))], axis=0)

    parts["sums"] = sums(P)
    parts["sums_meta"] = sums(META)
    k = np.arange(TOK)[None, :]
    parts["fox_mask"] = np.where(k <= P + META + p[:, None], 0.0, MASKED)
    sel = np.zeros((P, 30))
    sel[:64, 14], sel[64:, 15] = 1, 1
    parts["half_to_row"] = sel
    sel = np.zeros((P, 15))
    sel[:, 7] = 1
    parts["tile_to_row"] = sel
    parts["causal_tokens"] = s <= t
    dist = 255 - np.arange(SEQ + P - 1)
    n = np.maximum(dist, 0)
    exact = BUCKETS // 2
    nf = np.maximum(n, exact).astype(np.float32)
    large = exact + (np.log(nf / np.float32(exact)) / np.float32(math.log(MAX_DIST / exact))
                     * np.float32(BUCKETS - exact)).astype(np.int32)
    bucket = np.where(n < exact, n, np.minimum(large, BUCKETS - 1))
    hot = np.zeros((P, dist.size))
    hot[bucket, np.arange(dist.size)] = 1
    parts["bucket_hot"] = hot
    parts["line_mask"] = np.tile(np.where(dist >= 0, 0.0, MASKED), (P, 1))
    at, out = {}, []
    n = 0
    for name, a in parts.items():
        at[name] = (n, n + a.shape[1])
        out.append(a.astype(np.float32))
        n += a.shape[1]
    return np.concatenate(out, axis=1), at


class Order:

    def __init__(self, sem, steps):
        self.sem, self.steps, self.next = sem, {s: n + 1 for n, s in enumerate(steps)}, 0
        assert len(self.steps) == len(steps)

    def did(self, step):
        self.next += 1
        assert self.steps[step] == self.next, (step, self.steps[step], self.next)
        return self.sem, 1

    def after(self, step):
        return self.sem, self.steps[step]


class Linear:

    def __init__(self, iters, units, first_unit, first_tile, tiles_per_iter):
        self.iters, self.units = iters, units
        self.u0, self.t0, self.tiles = first_unit, first_tile, tiles_per_iter
        self.width = units[0](0).shape[2]
        self.extra = None
        self.u1 = first_unit + iters * len(units)
        self.t1 = first_tile + iters * tiles_per_iter


def transformer_pair_kernel(nc, a, out, table_at):
    ctx = ExitStack()
    with ctx:
        sb = lambda name, shape, dt=F32: ctx.enter_context(nc.sbuf_tensor(name, shape, dt))
        sem = lambda name: ctx.enter_context(nc.semaphore(name))

        w_raw = sb("w_raw", [P, RAW, UNIT_K, UNIT_C])
        w_hi = sb("w_hi", [P, 2, UNIT_K, UNIT_C], F32R)
        w_lo = sb("w_lo", [P, 2, UNIT_K, UNIT_C], F32R)
        act_hi = sb("act_hi", [P, KT, TOK], F32R)
        act_lo = sb("act_lo", [P, KT, TOK], F32R)
        res = sb("res", [P, KT, TOK])
        n_tab = max(e for n, (b, e) in table_at.items() if n not in ("bucket_hot", "line_mask"))
        tab = sb("tab", [P, n_tab])
        T = {n: tab[:, b:e] for n, (b, e) in table_at.items() if e <= n_tab}
        vec = sb("vec", [P, 2, P])
        rstd = sb("rstd", [P, TOK])
        inv = sb("inv", [P, TOK])
        ones = sb("ones", [P, P])
        lam = sb("lam", [P, 8])
        lam_in = sb("lam_in", [P, 4, QK])
        small = sb("small", [P, 64])
        small2 = sb("small2", [RHD, 2, TOK])
        half_a0 = sb("half_a0", [P, 8])
        f_bias = sb("f_bias", [P, 1])
        arena = sb("arena", [P, ARENA])
        psum = ctx.enter_context(nc.psum_tensor("psum", [P, 8, 512], F32))

        def area(at, *shape):
            n = int(np.prod(shape))
            v = arena[:, at:at + n]
            if len(shape) == 2:
                v = v.rearrange("p (a b) -> p a b", b=shape[1])
            elif len(shape) == 3:
                v = v.rearrange("p (a b c) -> p a b c", b=shape[1], c=shape[2])
            return v

        line_dram = nc.dram_tensor("bias_lines", [HEADS, P, SEQ + P], F32, kind="Internal").ap()

        ident = T["ident"]
        G_PRE, G_POST, G_FPRE, G_FPOST, G_CONV, W_CONV, G_SUBLN = 0, 16, 32, 48, 64, 72, 96
        (G_N1, G_N2, V_A0, V_KK, V_KA, V_RK, V_GNW, V_GNB, MU_RKV, MU_W, MU_A, MU_G, G_FQ,
         G_FK) = 0, 16, 32, 40, 48, 56, 64, 72, 80, 104, 105, 106, 108, 109

        def va(col):
            return vec[:, 0, col:col + 1]

        def vb(col):
            return vec[:, 1, col:col + 1]

        X = slice(META, TOK)

        def cols(w, kt0, col, step, width=UNIT_C):
            v = w.rearrange("(k p) n -> p k n", p=P)

            def src(i):
                c = bass.ds(col + step * i, width) if step else slice(col, col + width)
                return v[:, kt0:kt0 + UNIT_K, c]
            return src

        def rows(w, col):
            v = w.rearrange("(i k p) n -> p i k n", p=P, k=UNIT_K)

            def src(i):
                return v[:, bass.ds(i, 1), :, col:col + UNIT_C].rearrange("p i k n -> p (i k) n")
            return src

        w_in, w_out, w_down = a["w_in"][0], a["w_out"][0], a["w_down"][0]
        w_in2, w_o2 = a["w_in_2"][0], a["w_o_2"][0]
        w_a2, w_b2, w_gu2, w_down2 = (a["w_branch_a_2"][0], a["w_branch_b_2"][0],
                                      a["w_gate_up_2"][0], a["w_down_2"][0])
        full = range(0, KT, UNIT_K)
        W_OUT_K = (8, 12, 0, 4)
        plan = [
            ("w_in", 12, [cols(w_in, k, 0, UNIT_C) for k in full], 4),
            ("w_out", 4, [cols(w_out, k, 0, UNIT_C) for k in W_OUT_K], 4),
            ("ffn", 11, [cols(a["w_gate"][0], k, 0, UNIT_C) for k in full]
             + [cols(a["w_up"][0], k, 0, UNIT_C) for k in full], 8),
            ("down", 11, [rows(w_down, c * UNIT_C) for c in range(4)], 0),
            ("rkv", 6, [cols(w_in2, k, 0, UNIT_C) for k in full], 4),
            ("lora", 1, [cols(w_in2, k, 3072, 0, 448) for k in full], 4),
            ("fox", 6, [cols(w_in2, k, FOX0, UNIT_C) for k in full], 4),
            ("gates", 8, [cols(w_in2, k, GATE0, UNIT_C) for k in full], 4),
            ("branch", 4, [cols(w, k, 0, UNIT_C) for w in (w_a2, w_b2) for k in (0, 4)], 8),
            ("w_o", 4, [cols(w_o2, k, 0, UNIT_C) for k in full], 4),
            ("ffn2", 11, [cols(w_gu2, k, c, UNIT_C) for c in (0, FF) for k in full], 8),
            ("down2", 11, [rows(w_down2, c * UNIT_C) for c in range(4)], 0),
        ]
        L, u, t = {}, 0, 0
        for name, iters, units, tiles in plan:
            L[name] = Linear(iters, units, u, t, tiles)
            u, t = L[name].u1, L[name].t1
            if tiles == 0:
                t += KT
                L[name].t1 = t

        L["lora"].extra = [cols(w_in2, k, GATE0 - LANES, 0, 64) for k in full]
        L["lora"].width = UNIT_C

        raw_ready = [sem(f"raw_ready{n}") for n in range(RAW)]
        extra_ready = [sem(f"extra_ready{n}") for n in range(RAW)]
        hi_ready = sem("hi_ready")
        lo_ready = sem("lo_ready")
        unit_used = sem("unit_used")
        acc_done = sem("acc_done")
        acc_free = sem("acc_free")
        act_hi_ready = sem("act_hi_ready")
        act_lo_ready = sem("act_lo_ready")

        def repeat(eng, n, body):
            body(0)
            if n == 2:
                body(1)
            elif n > 2:
                with eng.Fori(1, n) as i:
                    body(i)

        def wait(eng, s, value):
            if not isinstance(value, int) or value > 0:
                eng.wait_ge(s, value)

        def stream_sp(lin):
            n = len(lin.units)

            def body(i):
                for s, src in enumerate(lin.units):
                    u = lin.u0 + n * i + s
                    w = src(i)
                    wait(nc.sync, lo_ready, 2 * (u - RAW + 1))
                    nc.sync.dma_start(w_raw[:, s % RAW, :, 0:w.shape[2]], w) \
                        .then_inc(raw_ready[s % RAW], 16)
                    if lin.extra:
                        nc.sync.dma_start(w_raw[:, s % RAW, :, w.shape[2]:lin.width], lin.extra[s](0)) \
                            .then_inc(extra_ready[s % RAW], 16)
            if lin.iters <= 4:
                for i in range(lin.iters):
                    body(i)
            else:
                repeat(nc.sync, lin.iters, body)

        def unit_hi(lin, i, s):
            n, wd = len(lin.units), lin.width
            u = lin.u0 + n * i + s
            nc.scalar.wait_ge(raw_ready[s % RAW], 16 * (lin.u0 // RAW + (n // RAW) * i + s // RAW + 1))
            if lin.extra:
                nc.scalar.wait_ge(extra_ready[s % RAW], 16)
            wait(nc.scalar, unit_used, u - 1)
            for h in range(2):
                nc.scalar.activation(w_hi[:, s % 2, 2 * h:2 * h + 2, 0:wd],
                                     w_raw[:, s % RAW, 2 * h:2 * h + 2, 0:wd],
                                     ACT.Copy).then_inc(hi_ready, 1)

        def unit_lo(lin, i, s):
            n, wd = len(lin.units), lin.width
            u = lin.u0 + n * i + s
            for h in range(2):
                nc.vector.wait_ge(hi_ready, 2 * u + h + 1)
                nc.vector.tensor_tensor(w_lo[:, s % 2, 2 * h:2 * h + 2, 0:wd],
                                        w_raw[:, s % RAW, 2 * h:2 * h + 2, 0:wd],
                                        w_hi[:, s % 2, 2 * h:2 * h + 2, 0:wd].bitcast(F32),
                                        ALU.subtract).then_inc(lo_ready, 1)

        def unit_mm(lin, i, s, tiles, k0, tok, start, stop, first_of_bank=None):
            pe = nc.tensor
            u = lin.u0 + len(lin.units) * i + s
            pe.wait_ge(lo_ready, 2 * u + 2)
            for m, (dst, c, wd, place) in enumerate(tiles):
                if start and place is not None and place >= 0:
                    wait(pe, acc_free, lin.t0 + lin.tiles * i + place - 3)
                for k in range(UNIT_K):
                    w1, w0 = w_hi[:, s % 2, k, c:c + wd], w_lo[:, s % 2, k, c:c + wd]
                    x1, x0 = act_hi[:, k0 + k, tok], act_lo[:, k0 + k, tok]
                    first = start and k == 0 and (first_of_bank is None or first_of_bank[m])
                    pe.matmul(dst, w1, x1, start=first, stop=False, skip_group_check=True)
                    pe.matmul(dst, w1, x0, start=False, stop=False, skip_group_check=True)
                    mm = pe.matmul(dst, w0, x1, start=False, stop=stop and k == UNIT_K - 1,
                                   skip_group_check=True)
                if m == len(tiles) - 1:
                    mm.then_inc(unit_used, 1)
                elif stop and place != -1:
                    mm.then_inc(acc_done, 1)

        def wait_tile(lin, i, g, m):
            if m == 3:
                size = len(lin.units) * 4 // max(lin.tiles, 4)
                nc.vector.wait_ge(unit_used, lin.u0 + len(lin.units) * i + size * (g + 1))
            else:
                nc.vector.wait_ge(acc_done, lin.t0 // 4 * 3 + lin.tiles // 4 * 3 * i + 3 * g + m + 1)

        def run_hooks(hooks, i, s):
            if isinstance(i, int) and i == 0:
                for f in hooks.get(s, ()):
                    f()

        def stream_act(lin, hooks={}, after_unit={}):
            def body(i):
                for s in range(len(lin.units)):
                    run_hooks(hooks, i, s)
                    unit_hi(lin, i, s)
                    if s in after_unit:
                        after_unit[s](i)
                run_hooks(hooks, i, len(lin.units))
            repeat(nc.scalar, lin.iters, body)

        def stream_dve(lin, evac, hooks={}):
            n, groups = len(lin.units), lin.tiles // 4
            size = n // groups

            def body(i):
                for s in range(n):
                    run_hooks(hooks, i, s)
                    unit_lo(lin, i, s)
                    if s % size == 0:
                        g = s // size - 1
                        if g >= 0:
                            evac(i, g)
                        elif not isinstance(i, int) or i > 0:
                            evac(i - 1, groups - 1)
                run_hooks(hooks, i, n)
            repeat(nc.vector, lin.iters, body)
            evac(lin.iters - 1, groups - 1)

        def stream_pe(lin, tok, hooks={}, widths=(P,) * 4, ks=None):
            n, groups = len(lin.units), lin.tiles // 4
            size = n // groups
            ntok = tok.stop - tok.start

            def body(i):
                for s in range(n):
                    run_hooks(hooks, i, s)
                    g, k = divmod(s, size)
                    c = np.cumsum((0,) + widths)
                    tiles = [(psum[0:widths[m], m, 0:ntok], int(c[m]), widths[m], 4 * g + m)
                             for m in range(4)]
                    if lin.extra:
                        tiles = [(psum[0:96, 4, 0:ntok], UNIT_C - 96, 96, -1)] + tiles
                    k0 = ks[s] if ks else UNIT_K * k
                    unit_mm(lin, i, s, tiles, k0, tok, k == 0, k == size - 1)
            repeat(nc.tensor, lin.iters, body)

        def down_steps(eng, steps, body):
            body(0, 0)
            with eng.Fori(1, steps - 2, 2) as i:
                body(i, 1)
                body(i + 1, 0)
            body(steps - 2, 1)
            body(steps - 1, 0)

        def down_act(lin, act_base):
            def body(i, slot):
                if isinstance(i, int) and i < 2:
                    nc.scalar.wait_ge(unit_used, lin.u0)
                else:
                    nc.scalar.wait_ge(unit_used, lin.u0 + 4 * (i - 1))
                if isinstance(i, int) and i == 0:
                    nc.scalar.wait_ge(*hid_ready(lin))
                nc.scalar.activation(act_hi[:, 4 * slot:4 * slot + 4, X], hid[:, bass.ds(4 * i, 4), :],
                                     ACT.Copy).then_inc(act_hi_ready, 1)
                for s in range(4):
                    unit_hi(lin, i, s)
            down_steps(nc.scalar, lin.iters, body)

        def down_dve(lin, act_base):
            def body(i, slot):
                nc.vector.wait_ge(act_hi_ready, act_base + i + 1)
                nc.vector.tensor_tensor(act_lo[:, 4 * slot:4 * slot + 4, X],
                                        hid[:, bass.ds(4 * i, 4), :],
                                        act_hi[:, 4 * slot:4 * slot + 4, X].bitcast(F32),
                                        ALU.subtract).then_inc(act_lo_ready, 1)
                for s in range(4):
                    unit_lo(lin, i, s)
            down_steps(nc.vector, lin.iters, body)

        def down_out(m):
            return psum[:, m // 2, (m % 2) * SEQ:(m % 2 + 1) * SEQ]

        def down_pe(lin, act_base):
            def body(i, slot):
                nc.tensor.wait_ge(act_lo_ready, act_base + i + 1)
                first = isinstance(i, int) and i == 0
                last = isinstance(i, int) and i == lin.iters - 1
                if first:
                    nc.tensor.wait_ge(acc_free, lin.t0)
                for s in range(4):
                    tiles = [(down_out(4 * s + m), m * P, P, None) for m in range(4)]
                    unit_mm(lin, i, s, tiles, 4 * slot, X, first, last, [True, False] * 2)
            down_steps(nc.tensor, lin.iters, body)

        hid = area(0, FT, SEQ)
        gate_n = area(FT * SEQ, 4, SEQ)
        gate_s = area(FT * SEQ + 4 * SEQ, 4, SEQ)
        up_n = area(FT * SEQ + 8 * SEQ, 4, SEQ)
        silu_done = sem("silu_done")
        hid_done = sem("hid_done")

        def hid_ready(lin):
            return hid_done, (L["ffn"].iters if lin is L["down"] else 2 * L["ffn"].iters)

        def take_tiles(lin, i, g, dst, op1=None):
            for m in range(4):
                wait_tile(lin, i, g, m)
                nc.vector.tensor_tensor(dst(m), psum[:, m, 0:SEQ], rstd[:, X], ALU.mult) \
                    .then_inc(acc_free, 1)

        def ffn_evac(lin, q):
            n = lin.iters * q

            def evac(i, g):
                if g == 0:
                    take_tiles(lin, i, 0, lambda m: gate_n[:, m])
                else:
                    take_tiles(lin, i, 1, lambda m: up_n[:, m])
                    nc.vector.wait_ge(silu_done, n + i + 1)
                    nc.vector.wait_ge(acc_free, lin.t0 + 8 * i + 8)
                    nc.vector.tensor_tensor(hid[:, bass.ds(4 * i, 4), :], gate_s, up_n, ALU.mult) \
                        .then_inc(hid_done, 1)
            return evac

        def ffn_silu(lin, q):
            def silu(i):
                nc.scalar.wait_ge(acc_free, lin.t0 + 8 * i + 4)
                nc.scalar.activation(gate_s, gate_n, ACT.Silu).then_inc(silu_done, 1)
            return {5: silu}

        SQ = area(14400, KT, TOK)
        sq_done, sums_done, mean_done, var_done, inv_done, rstd_done = (
            sem(n) for n in ("sq_done", "sums_done", "mean_done", "var_done", "inv_done", "rstd_done"))
        NORM = {n: q for q, n in enumerate(("pre", "post", "fpre", "fpost", "n1", "n2"))}
        INPUT_NORM = {n: q for q, n in enumerate(("pre", "fpre", "n1", "n2"))}
        sum_sq = sb("sum_sq", [P, TOK])

        def norm_square(name, tok):
            def f():
                nc.scalar.activation(SQ[:, :, 0:tok.stop - tok.start], res[:, :, tok],
                                     ACT.Square).then_inc(sq_done, 1)
            return f

        def norm_sum(name, tok):
            n = tok.stop - tok.start

            def f():
                nc.vector.wait_ge(sq_done, INPUT_NORM[name] + 1)
                nc.vector.tensor_reduce(sum_sq[:, 0:n], SQ[:, :, 0:n].rearrange("p k t -> p t k"),
                                        AX, ALU.add).then_inc(sums_done, 1)
            return f

        def norm_mean(name, tok):
            n = tok.stop - tok.start

            def f():
                nc.tensor.wait_ge(sums_done, INPUT_NORM[name] + 1)
                nc.tensor.matmul(psum[:, 4, 0:n], ones[:, :], sum_sq[:, 0:n], start=True, stop=True) \
                    .then_inc(mean_done, 1)
            return f

        def norm_inv(name, tok, bank=4):
            n = tok.stop - tok.start

            def f():
                nc.vector.wait_ge(mean_done, NORM[name] + 1)
                nc.vector.tensor_scalar(inv[:, tok], psum[:, bank, 0:n], 1.0 / D, RMS_EPS,
                                        ALU.mult, ALU.add).then_inc(var_done, 1)
                nc.vector.wait_ge(var_done, NORM[name] + 1)
                nc.vector.reciprocal(inv[:, tok], inv[:, tok]).then_inc(inv_done, 1)
            return f

        def norm_rstd(name, tok):
            def f():
                nc.scalar.wait_ge(inv_done, NORM[name] + 1)
                nc.scalar.activation(rstd[:, tok], inv[:, tok], ACT.Sqrt).then_inc(rstd_done, 1)
            return f

        ACT_BASE, at = {}, 0
        for n in ("w_in", "w_out", "ffn", "down", "rkv", "branch", "w_o", "ffn2", "down2"):
            ACT_BASE[n] = at
            at += L[n].iters if n.startswith("down") else KT
        PREV = {"w_out": "w_in", "ffn": "w_out", "rkv": "down", "branch": "gates", "w_o": "branch",
                "ffn2": "w_o"}

        def part_hi(name, src, k, tok, gain=None):
            if k == 0 and name in PREV:
                nc.scalar.wait_ge(unit_used, L[PREV[name]].u1)
            nc.scalar.activation(act_hi[:, k, tok], src, ACT.Copy,
                                 scale=1.0 if gain is None else gain).then_inc(act_hi_ready, 1)

        def part_lo(name, src, k, tok, gain=None):
            nc.vector.wait_ge(act_hi_ready, ACT_BASE[name] + k + 1)
            hi = act_hi[:, k, tok].bitcast(F32)
            if gain is None:
                nc.vector.tensor_tensor(act_lo[:, k, tok], src, hi, ALU.subtract) \
                    .then_inc(act_lo_ready, 1)
            else:
                nc.vector.scalar_tensor_tensor(out=act_lo[:, k, tok], in0=src, scalar=gain, in1=hi,
                                               op0=ALU.mult, op1=ALU.subtract) \
                    .then_inc(act_lo_ready, 1)

        def parts_wait(name, units=4, per=4):
            def hook(s):
                return lambda: nc.tensor.wait_ge(act_lo_ready, ACT_BASE[name] + per * (s + 1))
            return {s: [hook(s)] for s in range(units)}

        def both(*hooks):
            out = {}
            for h in hooks:
                for s, fs in h.items():
                    out.setdefault(s, []).extend(fs)
            return out

        f_out = area(0, KT, SEQ)
        f_sq = area(KT * SEQ, KT, SEQ)
        POST_BANK = (4, 0)
        f_n = area(2 * KT * SEQ, KT, SEQ)
        post_sq, post_scaled, post_added = sem("post_sq"), sem("post_scaled"), sem("post_added")

        def post_act(q, name, t0, nxt, gain_next, tok):
            for g in range(4):
                nc.scalar.wait_ge(acc_free, t0 + 4 * g + 4)
                nc.scalar.activation(f_sq[:, 4 * g:4 * g + 4], f_out[:, 4 * g:4 * g + 4],
                                     ACT.Square).then_inc(post_sq, 1)
            norm_rstd(name, X)()
            for k in range(KT):
                nc.scalar.wait_ge(post_added, KT * q + k + 1)
                part_hi(nxt, res[:, k, tok], k, tok, gain_next(k))

        def post_pe(q):
            for k in range(KT):
                nc.tensor.wait_ge(post_sq, 4 * q + k // 4 + 1)
                mm = nc.tensor.matmul(psum[:, POST_BANK[q], 0:SEQ], ones[:, :], f_sq[:, k], start=k == 0,
                                      stop=k == KT - 1)
            mm.then_inc(mean_done, 1)

        def post_dve(q, name, gain, nxt, gain_next, tok):
            norm_inv(name, X, bank=POST_BANK[q])()
            nc.vector.wait_ge(rstd_done, NORM[name] + 1)
            for k in range(KT + 3):
                if k < KT:
                    nc.vector.scalar_tensor_tensor(out=f_n[:, k], in0=f_out[:, k], scalar=gain(k),
                                                   in1=rstd[:, X], op0=ALU.mult, op1=ALU.mult) \
                        .then_inc(post_scaled, 1)
                if k >= 3:
                    part_lo(nxt, res[:, k - 3, tok], k - 3, tok, gain_next(k - 3))

        def post_pool(q):
            for k in range(KT):
                nc.gpsimd.wait_ge(post_scaled, KT * q + k + 1)
                nc.gpsimd.tensor_tensor(res[:, k, X], res[:, k, X], f_n[:, k], ALU.add) \
                    .then_inc(post_added, 1)

        def copy_tiles(lin, i, g, dst):
            for m in range(4):
                wait_tile(lin, i, g, m)
                nc.vector.tensor_copy(dst(m), psum[:, m, 0:SEQ]).then_inc(acc_free, 1)

        x_in = area(0, 2, D)
        meta_in = area(2 * D, D)
        line_tab = area(3 * D, 2, SEQ + P - 1)
        rows_in = area(3 * D + 800, 2, P)
        bias_in = area(3 * D + 800 + 256, HEADS)
        s_x, s_meta, s_tab, s_line, s_rows, s_lam = (
            sem(n) for n in ("x_loaded", "meta_loaded", "tables_loaded", "line_tables_loaded",
                             "rows_loaded", "lambda_loaded"))
        cleared = sem("cleared")
        start_pe = Order(sem("start_pe"), [("x", k) for k in range(KT)] + ["vec0", "vec1"]
                         + [("line", h) for h in range(HEADS)])
        start_act = Order(sem("start_act"), [("x", k) for k in range(1, KT, 2)]
                          + ["exp_lambda"])
        start_dve = Order(sem("start_dve"), [("x", k) for k in range(0, KT, 2)] + ["vec"]
                          + ["l_mul", "l_sum", "subln"]
                          + [("line", h) for h in range(HEADS)] + ["lambda"])
        lines_out, bias_loaded = sem("lines_out"), [sem("bias_loaded0"), sem("bias_loaded1")]
        ROWS = ([("norm_mix_pre", 0, G_PRE), ("norm_mix_post", 0, G_POST), ("norm_ffn_pre", 0, G_FPRE),
                 ("norm_ffn_post", 0, G_FPOST), ("conv_norm_gain", 0, G_CONV), ("conv_w", 0, W_CONV),
                 ("subln_gain", 0, G_SUBLN)]
                + [("norm1_g_2", 1, G_N1), ("norm2_g_2", 1, G_N2), ("rwkv_a0_2", 1, V_A0),
                   ("rwkv_k_k_2", 1, V_KK), ("rwkv_k_a_2", 1, V_KA), ("rwkv_r_k_2", 1, V_RK),
                   ("rwkv_gn_w_2", 1, V_GNW), ("rwkv_gn_b_2", 1, V_GNB)])

        def start_sp():
            sp = nc.sync
            sp.dma_start(x_in, a["x"][0].rearrange("(t p) d -> p t d", p=P)).then_inc(s_x, 16)
            sp.dma_start(tab[:, :], a["tables"][:, 0:n_tab]).then_inc(s_tab, 16)
            sp.wait_ge(cleared, 1)
            n = 0
            for name, g, r in ROWS:
                v = a[name][0]
                if len(v.shape) == 2 and v.shape[1] == RHD:
                    v = v.rearrange("(r t) d -> r (t d)", t=2)
                elif len(v.shape) == 2:
                    v = v.rearrange("c (r p) -> (c r) p", p=P)
                elif v.shape[0] > P:
                    v = v.rearrange("(r p) -> r p", p=P)
                else:
                    v = v.rearrange("(r p) -> r p", r=1)
                sp.dma_start(rows_in[r:r + v.shape[0], g, 0:v.shape[1]], v).then_inc(s_rows, 16)
                n += 1
            mu = a["rwkv_mu_2"][0]
            for r, c0, rows_n, width in ((MU_RKV, 0, 24, P), (MU_W, 3072, 1, LORA),
                                         (MU_A, 3072 + LORA, 1, LORA), (MU_G, 3072 + 2 * LORA, 2, P)):
                sp.dma_start(rows_in[r:r + rows_n, 1, 0:width],
                             mu[c0:c0 + rows_n * width].rearrange("(r p) -> r p", p=width)) \
                    .then_inc(s_rows, 16)
                n += 1
            for r, name in ((G_FQ, "fox_q_norm_g_2"), (G_FK, "fox_k_norm_g_2")):
                for h in range(2):
                    sp.dma_start(rows_in[r:r + 1, 1, h * RHD:(h + 1) * RHD], a[name]) \
                        .then_inc(s_rows, 16)
                    n += 1
            nc.start_rows = n
            sp.dma_start(meta_in[0:META], a["meta_tokens_2"]).then_inc(s_meta, 16)

        def start_sp_late():
            sp = nc.sync
            sp.dma_start(line_tab, a["line_tables"].rearrange("p (a n) -> p a n", a=2)) \
                .then_inc(s_line, 16)
            sp.dma_start(bias_in[0:BUCKETS, :], a["rel_bias"]).then_inc(s_line, 16)
            for n, name in enumerate(("lambda_q1", "lambda_k1", "lambda_q2", "lambda_k2")):
                sp.dma_start(lam_in[:, n, :], a[name].broadcast_to([P, QK])).then_inc(s_lam, 16)
        lines = area(3 * D + 800 + 256 + 8, HEADS, SEQ + P - 1)

        def start_pe_work():
            pe = nc.tensor
            pe.wait_ge(s_tab, 16)
            pe.wait_ge(s_x, 16)
            pe.wait_ge(s_meta, 16)
            for k in range(KT):
                if k >= 8:
                    o = start_act if k % 2 else start_dve
                    pe.wait_ge(*o.after(("x", k - 8)))
                c = slice(k * P, (k + 1) * P)
                pe.transpose(psum[:, k % 8, 0:META], meta_in[0:META, c], ident[0:META, 0:META])
                pe.transpose(psum[:, k % 8, META:META + P], x_in[:, 0, c], ident)
                pe.transpose(psum[:, k % 8, META + P:TOK], x_in[:, 1, c], ident) \
                    .then_inc(*start_pe.did(("x", k)))
            pe.wait_ge(s_rows, 16 * nc.start_rows)
            pe.wait_ge(*start_act.after(("x", 15)))
            pe.wait_ge(*start_dve.after(("x", 14)))
            for g in range(2):
                pe.transpose(psum[:, 4 + g, 0:P], rows_in[:, g], ident) \
                    .then_inc(*start_pe.did(f"vec{g}"))

        def start_lines_pe():
            pe = nc.tensor
            pe.wait_ge(s_line, 32)
            for h in range(HEADS):
                if h >= 2:
                    pe.wait_ge(*start_dve.after(("line", h - 2)))
                pe.matmul(psum[:, 6 + h % 2, 0:SEQ + P - 1],
                          bias_in[0:BUCKETS, h:h + 1].broadcast_to([BUCKETS, P]),
                          line_tab[0:BUCKETS, 0], start=True, stop=True) \
                    .then_inc(*start_pe.did(("line", h)))

        def start_act_work():
            for k in range(1, KT, 2):
                nc.scalar.wait_ge(*start_pe.after(("x", k)))
                nc.scalar.activation(res[:, k], psum[:, k % 8, 0:TOK], ACT.Copy) \
                    .then_inc(*start_act.did(("x", k)))

        def start_act_lambda():
            nc.scalar.wait_ge(*start_dve.after("l_sum"))
            nc.scalar.activation(lam[:, 2:4], lam[:, 0:2], ACT.Exp).then_inc(*start_act.did("exp_lambda"))

        def start_dve_work():
            v = nc.vector
            v.memset(rows_in, 0.0).then_inc(cleared, 1)
            v.memset(ones[:, :], 1.0)
            for k in range(0, KT, 2):
                v.wait_ge(*start_pe.after(("x", k)))
                v.tensor_copy(res[:, k], psum[:, k % 8, 0:TOK]).then_inc(*start_dve.did(("x", k)))
            v.wait_ge(*start_pe.after("vec1"))
            v.tensor_copy(vec[:, :, :], psum[:, 4:6, 0:P]).then_inc(*start_dve.did("vec"))

        def start_dve_lines():
            v = nc.vector
            v.wait_ge(s_lam, 64)
            v.tensor_tensor(lam_in[:, 0::2], lam_in[:, 0::2], lam_in[:, 1::2], ALU.mult) \
                .then_inc(*start_dve.did("l_mul"))
            v.wait_ge(*start_dve.after("l_mul"))
            v.tensor_reduce(lam[:, 0:2], lam_in[:, 0::2], AX, ALU.add) \
                .then_inc(*start_dve.did("l_sum"))
            v.tensor_scalar(lam[:, 5:6], va(G_SUBLN), 1.0 - LAMBDA_INIT, None, ALU.mult) \
                .then_inc(*start_dve.did("subln"))
            for h in range(HEADS):
                v.wait_ge(*start_pe.after(("line", h)))
                v.tensor_tensor(lines[:, h], psum[:, 6 + h % 2, 0:SEQ + P - 1], line_tab[:, 1],
                                ALU.add).then_inc(*start_dve.did(("line", h)))
            v.wait_ge(*start_act.after("exp_lambda"))
            v.scalar_tensor_tensor(out=lam[:, 4:5], in0=lam[:, 2:3], scalar=LAMBDA_INIT,
                                   in1=lam[:, 3:4], op0=ALU.add, op1=ALU.subtract) \
                .then_inc(*start_dve.did("lambda"))

        def start_sp_lines():
            nc.sync.wait_ge(*start_dve.after(("line", HEADS - 1)))
            nc.sync.dma_start(line_dram[:, :, 0:SEQ + P - 1].rearrange("h p n -> p h n"), lines) \
                .then_inc(lines_out, 16)

        proj = area(0, 6 * CT, SEQ)
        q_t, k_t, v_t, gb_t, gc_t, hc_t = (proj[:, CT * n:CT * (n + 1)] for n in range(6))
        v_tok = area(12288, 2, 1024)
        bias = area(14336, 2, SEQ)
        s_buf = area(14848, 2, 768)
        e_buf = area(16384, 2, 768)
        wt_buf = area(17920, 2, 384)
        H = HEADS
        at_pe_steps = [("v", n) for n in range(4)]
        at_act_steps = [("v", n) for n in range(4)]
        at_dve_steps = []
        for i in range(H + 1):
            at_pe_steps += [("scores", i)] * (i < H)
            at_pe_steps += [("wt", i - 1), ("o", i - 1)] * (i > 0)
            at_act_steps += [("exp", i)] * (i < H)
            at_act_steps += [("wt", i - 1), ("o", i - 1), ("osq", i - 1)] * (i > 0)
            if i < H:
                at_dve_steps += [(n, i) for n in ("s0", "s", "max0", "max", "neg", "conv1", "conv2",
                                                  "rsum", "rlam", "t0", "t", "w0", "w")]
        at_pe_steps += ["csum", "osum"] + [("spread", h) for h in range(H)]
        at_act_steps += ["csq", "crstd", "orstd"]
        at_dve_steps += ["cvar", "cinv", "ovar", "oinv"] + [("c", j) for j in range(CT)] \
            + [("a", j) for j in range(CT)]
        at_pe = Order(sem("attn_pe"), at_pe_steps)
        at_act = Order(sem("attn_act"), at_act_steps)
        at_dve = Order(sem("attn_dve"), at_dve_steps)
        at_pool = Order(sem("attn_pool"), ["z", "y", "c"])
        mx, sums, rs = small[:, 0:8], small[:, 8:16], small[:, 16:24]
        rows_sm = inv[0:H, 0:SEQ]

        def mixer_sp():
            nc.sync.wait_ge(lines_out, 16)
            for h in range(H):
                if h >= 2:
                    nc.sync.wait_ge(*at_dve.after(("s", h - 2)))
                line = line_dram[h]
                src = bass.AP(tensor=line.tensor, offset=line.offset + P - 1,
                              ap=[[SEQ + P - 1, P], [1, SEQ]])
                nc.sync.dma_start(bias[:, h % 2], src).then_inc(bias_loaded[h % 2], 16)

        def mixer_pe():
            pe = nc.tensor
            pe.wait_ge(acc_free, L["w_in"].t1)
            for n in range(4):
                for j in range(4):
                    b, h = divmod(4 * n + j, H)
                    mm = pe.transpose(psum[:, 4 + n, j * P:(j + 1) * P], v_t[:, h, b * P:(b + 1) * P], ident)
                mm.then_inc(*at_pe.did(("v", n)))
            for i in range(H + 1):
                if i < H:
                    if i >= 2:
                        pe.wait_ge(*at_dve.after(("s", i - 2)))
                    for b in range(2):
                        for c in range(2):
                            r = slice(c * QK, (c + 1) * QK)
                            n = P * (b + 1)
                            mm = pe.matmul(psum[:, 2 * (i % 2) + c, P * b:P * b + n],
                                           q_t[r, i, b * P:(b + 1) * P], k_t[r, i, 0:n],
                                           start=True, stop=True)
                    mm.then_inc(*at_pe.did(("scores", i)))
                if i > 0:
                    h = i - 1
                    pe.wait_ge(*at_dve.after(("w", h)))
                    if h == 0:
                        pe.wait_ge(*at_act.after(("v", 3)))
                    if h >= 2:
                        pe.wait_ge(*at_act.after(("osq", h - 2)))
                    w = s_buf[:, h % 2]
                    wt = psum[:, 4 + h % 2]
                    pe.transpose(wt[:, 0:P], w[:, 0:P], ident)
                    pe.transpose(wt[:, P:2 * P], w[:, P:2 * P], ident)
                    pe.transpose(wt[:, 2 * P:3 * P], w[:, 2 * P:3 * P], ident) \
                        .then_inc(*at_pe.did(("wt", h)))
                    pe.wait_ge(*at_act.after(("wt", h)))
                    o, ws = psum[:, 6 + h % 2], wt_buf[:, h % 2]
                    hc = slice(h * P, (h + 1) * P)
                    pe.matmul(o[:, 0:SEQ], v_tok[:, 0, hc], ws[:, 0:SEQ], start=True, stop=False,
                              skip_group_check=True)
                    pe.matmul(o[:, P:SEQ], v_tok[:, 1, hc], ws[:, SEQ:SEQ + P], start=False,
                              stop=True, skip_group_check=True).then_inc(*at_pe.did(("o", h)))
            pe.wait_ge(*at_act.after("csq"))
            for j in range(CT):
                mm = pe.matmul(psum[:, 0, 0:SEQ], ones[:, :], gc_t[:, j], start=j == 0, stop=j == CT - 1)
            mm.then_inc(*at_pe.did("csum"))
            for h in range(H):
                mm = pe.matmul(psum[0:H, 1, 0:SEQ], T["tile_to_row"][:, 7 - h:15 - h], k_t[:, h],
                               start=h == 0, stop=h == H - 1)
            mm.then_inc(*at_pe.did("osum"))
            pe.wait_ge(*at_act.after("orstd"))
            for h in range(H):
                if h >= 4:
                    pe.wait_ge(*at_dve.after(("a", h - 4)))
                pe.matmul(psum[:, 2 + h % 4, 0:SEQ], ident[0:H, h:h + 1].broadcast_to([H, P]),
                          rows_sm, start=True, stop=True).then_inc(*at_pe.did(("spread", h)))

        def mixer_act():
            s = nc.scalar
            for n in range(4):
                s.wait_ge(*at_pe.after(("v", n)))
                s.activation(v_tok[:, n // 2, (n % 2) * 512:(n % 2 + 1) * 512], psum[:, 4 + n, :],
                             ACT.Copy).then_inc(*at_act.did(("v", n)))
            for i in range(H + 1):
                if i < H:
                    s.wait_ge(*at_dve.after(("neg", i)))
                    if i >= 2:
                        s.wait_ge(*at_dve.after(("w", i - 2)))
                    for r in range(4):
                        b, c = divmod(r, 2)
                        n = P * (b + 1)
                        col = slice(2 * P * b + c * n, 2 * P * b + (c + 1) * n)
                        mm = s.activation(e_buf[:, i % 2, col], s_buf[:, i % 2, col], ACT.Exp,
                                          bias=mx[:, 4 * (i % 2) + r:4 * (i % 2) + r + 1],
                                          accum_out=sums[:, 4 * (i % 2) + r:4 * (i % 2) + r + 1])
                    mm.then_inc(*at_act.did(("exp", i)))
                if i > 0:
                    h = i - 1
                    s.wait_ge(*at_pe.after(("wt", h)))
                    s.activation(wt_buf[:, h % 2], psum[:, 4 + h % 2, 0:384], ACT.Copy) \
                        .then_inc(*at_act.did(("wt", h)))
                    s.wait_ge(*at_pe.after(("o", h)))
                    s.activation(q_t[:, h], psum[:, 6 + h % 2, 0:SEQ], ACT.Copy) \
                        .then_inc(*at_act.did(("o", h)))
                    s.activation(k_t[:, h], psum[:, 6 + h % 2, 0:SEQ], ACT.Square) \
                        .then_inc(*at_act.did(("osq", h)))
            s.wait_ge(*at_pool.after("c"))
            s.activation(gc_t, gb_t, ACT.Square).then_inc(*at_act.did("csq"))
            s.wait_ge(*at_dve.after("cinv"))
            s.activation(rstd[:, X], inv[:, X], ACT.Sqrt).then_inc(*at_act.did("crstd"))
            s.wait_ge(*at_dve.after("oinv"))
            s.activation(rows_sm, rows_sm, ACT.Sqrt).then_inc(*at_act.did("orstd"))
            for n, (o, j) in enumerate([("c", j) for j in range(CT)] + [("a", j) for j in range(CT)]):
                s.wait_ge(*at_dve.after((o, j)))
                if o == "c":
                    part_hi("w_out", hc_t[:, j], CT + j, X) if n else part_hi0("w_out", hc_t[:, j], CT + j)
                else:
                    part_hi("w_out", v_t[:, j], j, X)

        def part_hi0(name, src, k):
            nc.scalar.wait_ge(unit_used, L[PREV[name]].u1)
            nc.scalar.activation(act_hi[:, k, X], src, ACT.Copy).then_inc(act_hi_ready, 1)

        def mixer_dve():
            v = nc.vector
            for i in range(H):
                v.wait_ge(*at_pe.after(("scores", i)))
                v.wait_ge(bias_loaded[i % 2], 16 * (i // 2 + 1))
                if i >= 2:
                    v.wait_ge(*at_pe.after(("wt", i - 2)))
                q = 4 * (i % 2)
                sb_, eb = s_buf[:, i % 2], e_buf[:, i % 2]
                s0 = sb_[:, 0:256].rearrange("p (c k) -> p c k", c=2)
                s1 = sb_[:, 256:768].rearrange("p (c k) -> p c k", c=2)
                pair = psum[:, 2 * (i % 2):2 * (i % 2) + 2]
                p0 = pair[:, :, 0:P]
                p1 = pair[:, :, P:P + SEQ]
                b1 = bias[:, i % 2].unsqueeze(1)
                v.scalar_tensor_tensor(out=s0, in0=p0, scalar=QK ** -0.5,
                                       in1=b1[:, :, P:SEQ].broadcast_to([P, 2, P]),
                                       op0=ALU.mult, op1=ALU.add).then_inc(*at_dve.did(("s0", i)))
                v.scalar_tensor_tensor(out=s1, in0=p1, scalar=QK ** -0.5,
                                       in1=b1.broadcast_to([P, 2, SEQ]),
                                       op0=ALU.mult, op1=ALU.add).then_inc(*at_dve.did(("s", i)))
                v.wait_ge(*at_dve.after(("s0", i)))
                v.tensor_reduce(mx[:, q:q + 2], s0, AX, ALU.max).then_inc(*at_dve.did(("max0", i)))
                v.wait_ge(*at_dve.after(("s", i)))
                v.tensor_reduce(mx[:, q + 2:q + 4], s1, AX, ALU.max) \
                    .then_inc(*at_dve.did(("max", i)))
                v.wait_ge(*at_dve.after(("max", i)))
                v.tensor_scalar(mx[:, q:q + 4], mx[:, q:q + 4], -1.0, None, ALU.mult) \
                    .then_inc(*at_dve.did(("neg", i)))
                if i == 0:
                    v.wait_ge(*at_pool.after("y"))
                for tap in (1, 2):
                    if tap == 2:
                        v.wait_ge(*at_dve.after(("conv1", i)))
                    v.scalar_tensor_tensor(out=gc_t[:, i, tap:SEQ], in0=hc_t[:, i, 0:SEQ - tap],
                                           scalar=va(W_CONV + CT * (2 - tap) + i),
                                           in1=gc_t[:, i, tap:SEQ], op0=ALU.mult, op1=ALU.add) \
                        .then_inc(*at_dve.did((f"conv{tap}", i)))
                v.wait_ge(*at_act.after(("exp", i)))
                v.reciprocal(rs[:, q:q + 4], sums[:, q:q + 4]).then_inc(*at_dve.did(("rsum", i)))
                v.wait_ge(*at_dve.after(("rsum", i)))
                v.tensor_scalar(rs[:, q + 1:q + 4:2], rs[:, q + 1:q + 4:2], lam[:, 4:5], None,
                                ALU.mult).then_inc(*at_dve.did(("rlam", i)))
                v.wait_ge(*at_dve.after(("rlam", i)))
                v.tensor_scalar(eb[:, P:2 * P], eb[:, P:2 * P], rs[:, q + 1:q + 2], None, ALU.mult) \
                    .then_inc(*at_dve.did(("t0", i)))
                v.tensor_scalar(eb[:, 512:768], eb[:, 512:768], rs[:, q + 3:q + 4], None, ALU.mult) \
                    .then_inc(*at_dve.did(("t", i)))
                v.wait_ge(*at_dve.after(("t0", i)))
                v.scalar_tensor_tensor(out=sb_[:, 0:P], in0=eb[:, 0:P], scalar=rs[:, q:q + 1],
                                       in1=eb[:, P:2 * P], op0=ALU.mult, op1=ALU.subtract) \
                    .then_inc(*at_dve.did(("w0", i)))
                v.wait_ge(*at_dve.after(("t", i)))
                v.scalar_tensor_tensor(out=sb_[:, P:3 * P], in0=eb[:, 256:512],
                                       scalar=rs[:, q + 2:q + 3],
                                       in1=eb[:, 512:768], op0=ALU.mult, op1=ALU.subtract) \
                    .then_inc(*at_dve.did(("w", i)))
            v.wait_ge(*at_pe.after("csum"))
            v.tensor_scalar(inv[:, X], psum[:, 0, 0:SEQ], 1.0 / 1024, RMS_EPS, ALU.mult, ALU.add) \
                .then_inc(*at_dve.did("cvar"))
            v.wait_ge(*at_dve.after("cvar"))
            v.reciprocal(inv[:, X], inv[:, X]).then_inc(*at_dve.did("cinv"))
            v.wait_ge(*at_pe.after("osum"))
            v.wait_ge(*at_act.after("crstd"))
            v.tensor_scalar(rows_sm, psum[0:H, 1, 0:SEQ], 1.0 / HD, SUBLN_EPS, ALU.mult, ALU.add) \
                .then_inc(*at_dve.did("ovar"))
            v.wait_ge(*at_dve.after("ovar"))
            v.reciprocal(rows_sm, rows_sm).then_inc(*at_dve.did("oinv"))
            for j in range(CT + 3):
                if j < CT:
                    v.scalar_tensor_tensor(out=hc_t[:, j], in0=gb_t[:, j], scalar=va(G_CONV + j),
                                           in1=rstd[:, X], op0=ALU.mult, op1=ALU.mult) \
                        .then_inc(*at_dve.did(("c", j)))
                if j >= 3:
                    part_lo_n("w_out", hc_t[:, j - 3], CT + j - 3, j - 3)
            for j in range(CT + 3):
                if j < CT:
                    v.wait_ge(*at_pe.after(("spread", j)))
                    v.scalar_tensor_tensor(out=v_t[:, j], in0=q_t[:, j], scalar=lam[:, 5:6],
                                           in1=psum[:, 2 + j % 4, 0:SEQ], op0=ALU.mult,
                                           op1=ALU.mult).then_inc(*at_dve.did(("a", j)))
                if j >= 3:
                    part_lo_n("w_out", v_t[:, j - 3], j - 3, CT + j - 3)

        def part_lo_n(name, src, k, nth):
            nc.vector.wait_ge(act_hi_ready, ACT_BASE[name] + nth + 1)
            nc.vector.tensor_tensor(act_lo[:, k, X], src, act_hi[:, k, X].bitcast(F32),
                                    ALU.subtract).then_inc(act_lo_ready, 1)

        def mixer_pool():
            g = nc.gpsimd
            g.wait_ge(acc_free, L["w_in"].t1)
            g.tensor_tensor(hc_t, gc_t, hc_t, ALU.mult).then_inc(*at_pool.did("z"))
            g.wait_ge(*at_pool.after("z"))
            w2 = vec[:, 0, W_CONV + 2 * CT:W_CONV + 3 * CT].unsqueeze(2).broadcast_to([P, CT, SEQ])
            g.tensor_tensor(gc_t, hc_t, w2, ALU.mult).then_inc(*at_pool.did("y"))
            g.wait_ge(*at_dve.after(("conv2", H - 1)))
            g.tensor_tensor(gb_t, gc_t, gb_t, ALU.mult).then_inc(*at_pool.did("c"))

        def stream_sp_first(lin, between):
            n = len(lin.units)

            def body(i):
                for s, src in enumerate(lin.units):
                    u = lin.u0 + n * i + s
                    w = src(i)
                    wait(nc.sync, lo_ready, 2 * (u - RAW + 1))
                    nc.sync.dma_start(w_raw[:, s % RAW, :, :], w).then_inc(raw_ready[s % RAW], 16)
            body(0)
            between()
            with nc.sync.Fori(1, lin.iters) as i:
                body(i)

        def down_sp(lin):
            def body(i):
                for s, src in enumerate(lin.units):
                    w = src(i)
                    nc.sync.wait_ge(lo_ready, 2 * (lin.u0 + 4 * i + s - RAW + 1))
                    nc.sync.dma_start(w_raw[:, s % RAW, :, :], w).then_inc(raw_ready[s % RAW], 16)
            with nc.sync.Fori(0, lin.iters) as i:
                body(i)

        def down_copy(lin):
            for m in range(KT):
                s, last = m // 4, m | 1
                if last % 4 == 3:
                    nc.vector.wait_ge(unit_used, lin.u1 - 3 + s)
                else:
                    nc.vector.wait_ge(acc_done, lin.t0 // 4 * 3 + 3 * s + last % 4 + 1)
                nc.vector.tensor_copy(f_out[:, m], down_out(m)).then_inc(acc_free, 1)
        ALL = slice(0, TOK)
        PIECES = [slice(0, META), slice(META, META + P), slice(META + P, TOK)]
        BLOCK2_IN = ("rkv", lambda k: vb(G_N1 + k), ALL)

        def take(lin, i, g, dst, tok, widths=(P,) * 4):
            n = tok.stop - tok.start
            for m in range(4):
                wait_tile(lin, i, g, m)
                w = widths[m]
                nc.vector.tensor_tensor(dst(m)[0:w], psum[0:w, m, 0:n], rstd[0:w, tok], ALU.mult) \
                    .then_inc(acc_free, 1)

        ZP = TOK + 1
        z = area(0, 28, ZP)
        at0 = 28 * ZP

        def place(*shape):
            nonlocal at0
            v = area(at0, *shape)
            at0 += int(np.prod(shape))
            return v

        w2s, a2s, g2s = place(2, P), place(2, P), place(2, 2 * P)
        tw, sg = place(TOK), place(2, SEQ)
        diff, shift = place(2, TOK), place(TOK)
        a_t, kf, kkn = place(TOK), place(TOK), place(TOK)
        ar = place(2, TOK)
        einv, bh, kh = place(TOK), place(TOK), place(TOK)
        ld = place(3, P)
        toks = place(4, P)
        tokm = place(3, P)
        gm = place(4, 4 * P)
        gm0 = place(2, 2 * META)
        inv_s = [place(4, P) for _ in range(6)]
        inv_m = [place(2, META) for _ in range(6)]
        state, state_h = place(RHD), place(RHD)
        xs, us = (diff[:, 1, n * P:(n + 1) * P].rearrange("p (h v) -> p h v", h=2) for n in range(2))
        ys = shift[:, 0:SEQ]
        eaux = place(9)
        assert at0 <= ARENA, at0
        y_sq = gm.rearrange("p q (a t) -> p (q a) t", a=2)
        rows_kk = small2[0:LANES, 0]

        def zt(n):
            return z[:, n, 1:ZP]

        lora_w = (LORA, LORA, P, P)
        loaded_w2 = [sem("lora_slices0"), sem("lora_slices1")]
        fox_bias_loaded = sem("fox_bias_loaded")
        rw_dve_steps = ["zero", "ones_row", "gm_zero"]
        Z_ORDER = [24, 25, 26, 27] + [n for j in range(8) for n in (8 + j, j, 16 + j)]
        for q in range(len(Z_ORDER) + 1):
            rw_dve_steps += [("d", n) for n in Z_ORDER[q:q + 1]] + [("z", n) for n in Z_ORDER[q - 1:q] if q]
        rw_dve_steps += ["kkvar", "kkinv"]
        INVERSE = [["n8"], ["nt8"], ["int8"], ["p2", "ip2", "p2t"], ["ip4", "r1t"], ["nm16"], ["r", "rt"]]
        for m in (16, 32, 64):
            INVERSE += [[f"p{m}"]] + [[f"nm{2 * m}"]] * (m < 64) + [[f"r{m}", f"rt{m}"]]
        INVERSE += [["p128"], ["r128"]]
        INVERSE = [(n, h) for stage in INVERSE for h in range(2) for n in stage]
        for j in range(8):
            rw_dve_steps += [(n, j) for n in ["ld", "a", "t1", "kf", "kkn", "rk", "b", "bh", "kh", "ah", "rh",
                                              "bv", "gram", "gram0"] + INVERSE
                             + ["x0", "u0", "s0", "sh1", "x1", "u1", "sd", "s1", "sh2", "x2", "u2",
                                "ys", "yc"]]
        rw_dve_steps += ["yvar", "yinv"]
        for j in range(8):
            rw_dve_steps += [("y1", j), ("y2", j), ("y3", j)]
        rw_act_steps = ["tanh", "sigm"] + [("kksq", j) for j in range(8)] + ["kkr"]
        for j in range(8):
            rw_act_steps += [(n, j) for n in ("ld", "a", "exp", "toks")]
        rw_act_steps += ["ysq", "yr"]
        rw_pe_steps = ["kksum"]
        PE_INV = ["nt", "p2", "p4", "r"]
        for m in (16, 32, 64, 128):
            PE_INV += [f"p{m}", f"d{m}"]
        PE_INV = [(n, h) for n in PE_INV for h in range(2)]
        for j in range(8):
            rw_pe_steps += [(n, j) for n in ["logits", "kkspread", "sums", "bonus", "toks", "gram"] + PE_INV
                            + ["x0", "u0", "s0", "x1", "u1", "y1s1", "x2", "u2", "y2", "yc"]]
        rw_pe_steps += ["ysum"] + [("out", j) for j in range(8)]
        rd, ra, rp = (Order(sem(n), s) for n, s in (("rwkv_dve", rw_dve_steps), ("rwkv_act", rw_act_steps),
                                                    ("rwkv_pe", rw_pe_steps)))

        def rwkv_sp():
            nc.sync.dma_start(f_bias[32:32 + LANES, :], a["fox_f_bias_2"].rearrange("a h -> h a")) \
                .then_inc(fox_bias_loaded, 16)
            w2, a2, g2, w0 = a["rwkv_w2_2"][0], a["rwkv_a2_2"][0], a["rwkv_g2_2"][0], a["rwkv_w0_2"]
            for j in range(8):
                b, c = j % 2, slice(j * P, (j + 1) * P)
                if j >= 2:
                    nc.sync.wait_ge(*rp.after(("logits", j - 2)))
                nc.sync.dma_start(w2s[0:LORA, b], w2[:, c]).then_inc(loaded_w2[b], 16)
                nc.sync.dma_start(w2s[LORA:LORA + 1, b], w0[:, c]).then_inc(loaded_w2[b], 16)
                nc.sync.dma_start(a2s[0:LORA, b], a2[:, c]).then_inc(loaded_w2[b], 16)
            for j in range(8):
                b, c = j % 2, slice(j * P, (j + 1) * P)
                if j >= 2:
                    nc.sync.wait_ge(*rp.after(("out", j - 2)))
                nc.sync.dma_start(g2s[:, b].rearrange("p (c n) -> p c n", c=2),
                                  g2[:, c].rearrange("(c p) n -> p c n", p=P)).then_inc(loaded_g2[b], 16)

        flk = small2[:, 0]
        loaded_g2 = [sem("g2_slices0"), sem("g2_slices1")]

        def sl(n, q, meta):
            if meta:
                return inv_m[n][0:META, q, :]
            return inv_s[n][:, q, :]

        def n_of(q, meta):
            return gm0[0:META, q, 0:META] if meta else gm[:, q, 0:P]

        def ps(bank, q, meta):
            if meta:
                return psum[0:META, 2 * q + bank, 2 * P:2 * P + META]
            return psum[:, 2 * (q // 2) + bank, (q % 2) * P:(q % 2 + 1) * P]

        def rwkv_pe():
            pe = nc.tensor
            for j in range(8):
                pe.wait_ge(*ra.after(("kksq", j)))
                mm = pe.matmul(psum[0:LANES, 0, 0:TOK], T["half_to_row"][:, 14 - 2 * j:30 - 2 * j],
                               diff[:, j % 2], start=j == 0, stop=j == 7)
                if j == 7:
                    mm.then_inc(*rp.did("kksum"))
                else:
                    mm.then_inc(kk_used, 1)
            for j in range(8):
                b = j % 2
                pe.wait_ge(loaded_w2[b], 48 * (j // 2 + 1))
                if j == 0:
                    pe.wait_ge(*ra.after("tanh"))
                    pe.wait_ge(*rd.after("kkvar"))
                    pe.wait_ge(*rd.after(("z", 25)))
                else:
                    pe.wait_ge(*rd.after(("yc", j - 1)))
                for n, t in enumerate(PIECES):
                    rows = t.stop - t.start
                    pe.matmul(psum[0:rows, 0, n * P:(n + 1) * P], tw[0:LORA + 1, t], w2s[0:LORA + 1, b],
                              start=True, stop=True)
                pe.matmul(psum[:, 1, 0:TOK], a2s[0:LORA, b], z[0:LORA, 25, 1:ZP], start=True, stop=True) \
                    .then_inc(*rp.did(("logits", j)))
                if j == 0:
                    pe.wait_ge(*ra.after("kkr"))
                for h in range(2):
                    mm = pe.matmul(psum[h * RHD:(h + 1) * RHD, 2, 0:TOK],
                                   ident[0:LANES, 2 * j + h:2 * j + h + 1].broadcast_to([LANES, RHD]),
                                   rows_kk, start=True, stop=True)
                mm.then_inc(*rp.did(("kkspread", j)))
                pe.wait_ge(*rd.after(("ld", j)))
                for n, t in enumerate(PIECES):
                    rows = t.stop - t.start
                    tb = T["sums_meta" if n == 0 else "sums"]
                    lhs = ld[0:rows, n, :]
                    pe.matmul(psum[:, 4, t], lhs, tb[0:rows, 0:rows], start=True, stop=True)
                    pe.matmul(psum[:, 3, t], lhs, tb[0:rows, rows:2 * rows], start=True, stop=True)
                    mm = pe.matmul(psum[:, 5, 3 * n:3 * n + 3], lhs, tb[0:rows, 2 * rows:2 * rows + 3],
                                   start=True, stop=True)
                mm.then_inc(*rp.did(("sums", j)))
                pe.wait_ge(*rd.after(("rk", j)))
                pe.matmul(psum[:, 0, 0:TOK], T["head_sum"], diff[:, 0], start=True, stop=True) \
                    .then_inc(*rp.did(("bonus", j)))
                pe.wait_ge(*rd.after(("kh", j)))
                c1 = PIECES[1]
                for n, src in enumerate((bh[:, c1], kh[:, c1], zt(16 + j)[:, c1], zt(16 + j)[:, PIECES[2]])):
                    pe.transpose(psum[:, 6, n * P:(n + 1) * P], src, ident)
                for n, src in enumerate((bh[:, 0:META], kh[:, 0:META], zt(16 + j)[:, 0:META])):
                    mm = pe.transpose(psum[0:META, 7, n * P:(n + 1) * P], src, ident)
                mm.then_inc(*rp.did(("toks", j)))
                pe.wait_ge(*rd.after(("bv", j)))
                pe.wait_ge(*ra.after(("exp", j)))
                for h in range(2):
                    r = slice(h * RHD, (h + 1) * RHD)
                    for c in range(2):
                        t0 = META + c * P
                        q = 2 * h + c
                        for n, src in enumerate((bh, kh)):
                            o = 2 * P * n
                            pe.matmul(psum[0:64, q, o:o + 2 * P].rearrange("p (a t) -> p a t", a=2),
                                      src[r, t0:t0 + 64], ar[r, :, t0:t0 + P], start=True, stop=True)
                            pe.matmul(psum[64:P, q, o:o + 2 * P].rearrange("p (a t) -> p a t", a=2)[:, :, 64:P],
                                      src[r, t0 + 64:t0 + P], ar[r, :, t0 + 64:t0 + P],
                                      start=True, stop=True)
                    for n, src in enumerate((bh, kh)):
                        mm = pe.matmul(psum[0:META, 4 + h, n * META:(n + 1) * META], src[r, 0:META],
                                       ar[r, 0, 0:META], start=True, stop=True)
                mm.then_inc(*rp.did(("gram", j)))

                pe.wait_ge(*rd.after(("gram0", j)))

                def of_head(h, meta, f):
                    for q in (2 * h, 2 * h + 1):
                        last = f(q, False)
                    return f(h, True) if meta else last

                for h in range(2):
                    of_head(h, True, lambda q, m: pe.transpose(
                        ps(0, q, m), n_of(q, m), ident[0:META, 0:META] if m else ident)) \
                        .then_inc(*rp.did((("nt", h), j)))

                def products(name, wait_for, pairs, meta=True):
                    for h in range(2):
                        pe.wait_ge(*rd.after(((wait_for, h), j)))
                        for bank, (l, r_) in enumerate(pairs):
                            last = of_head(h, meta, lambda q, m: pe.matmul(
                                ps(bank, q, m), sl(l, q, m), sl(r_, q, m), start=True, stop=True))
                        last.then_inc(*rp.did(((name, h), j)))

                products("p2", "nt8", ((0, 2), (2, 0)))
                products("p4", "p2t", ((4, 3), (5, 1)))
                products("r", "r1t", ((4, 3), (3, 4)))
                for m in (16, 32, 64):
                    products(f"p{m}", "rt" if m == 16 else f"rt{m // 2}", ((2, 1),), m == 16)
                    products(f"d{m}", f"p{m}", ((3, 0), (0, 3)), m == 16)
                for h in range(2):
                    pe.wait_ge(*rd.after((("rt64", h), j)))
                    for q in (2 * h, 2 * h + 1):
                        mm = pe.matmul(ps(0, q, False)[64:P, 0:64], gm[0:64, q, 64:P],
                                       inv_s[1][0:64, q, 0:64], start=True, stop=True)
                    mm.then_inc(*rp.did((("p128", h), j)))
                for h in range(2):
                    pe.wait_ge(*rd.after((("p128", h), j)))
                    for q in (2 * h, 2 * h + 1):
                        mm = pe.matmul(ps(1, q, False)[0:64, 0:64], inv_s[3][64:P, q, 0:64],
                                       inv_s[0][64:P, q, 64:P], start=True, stop=True)
                    mm.then_inc(*rp.did((("d128", h), j)))

                hs = [slice(h * RHD, (h + 1) * RHD) for h in range(2)]
                pe.wait_ge(*rd.after((("r128", 1), j)))
                pe.wait_ge(*ra.after(("toks", j)))
                for h in range(2):
                    mm = pe.matmul(psum[0:META, 0, hs[h]], gm0[0:META, h, META:2 * META],
                                   tokm[0:META, 2, hs[h]], start=True, stop=True)
                mm.then_inc(*rp.did(("x0", j)))
                pe.wait_ge(*rd.after(("x0", j)))
                for h in range(2):
                    mm = pe.matmul(psum[0:META, 1, hs[h]], inv_m[0][0:META, h, :], xs[0:META, h],
                                   start=True, stop=True)
                mm.then_inc(*rp.did(("u0", j)))
                pe.wait_ge(*rd.after(("u0", j)))
                for h in range(2):
                    o = psum[hs[h], 2, 0:RHD]
                    pe.matmul(o, tokm[0:META, 0, hs[h]], us[0:META, h], start=True, stop=False)
                    mm = pe.matmul(o, tokm[0:META, 1, hs[h]], tokm[0:META, 2, hs[h]], start=False, stop=True)
                mm.then_inc(*rp.did(("s0", j)))
                for c in range(2):
                    t = PIECES[c + 1]
                    vtok = toks[:, 2 + c]
                    pe.wait_ge(*rd.after((f"sh{c + 1}", j)))
                    for h in range(2):
                        o = psum[:, h, 0:RHD]
                        pe.matmul(o, gm[:, 2 * h + c, 2 * P:3 * P], vtok[:, hs[h]], start=True, stop=False)
                        mm = pe.matmul(o, ar[hs[h], 0, t], state_h[hs[h], :], start=False, stop=True)
                    mm.then_inc(*rp.did((f"x{c + 1}", j)))
                    pe.wait_ge(*rd.after((f"x{c + 1}", j)))
                    for h in range(2):
                        mm = pe.matmul(psum[:, 3, hs[h]], inv_s[0][:, 2 * h + c, :], xs[:, h],
                                       start=True, stop=True)
                    mm.then_inc(*rp.did((f"u{c + 1}", j)))
                    pe.wait_ge(*rd.after((f"u{c + 1}", j)))
                    for h in range(2):
                        o = psum[hs[h], 4 + c, 0:P]
                        pe.matmul(o, us[:, h], gm[:, 2 * h + c, P:2 * P], start=True, stop=False)
                        pe.matmul(o, vtok[:, hs[h]], gm[:, 2 * h + c, 3 * P:4 * P], start=False, stop=False)
                        mm = pe.matmul(o, state_h[hs[h], :], ar[hs[h], 1, t], start=False, stop=True)
                    if c == 0:
                        for h in range(2):
                            o = psum[hs[h], 6, 0:RHD]
                            pe.matmul(o, toks[:, 0, hs[h]], us[:, h], start=True, stop=False)
                            mm = pe.matmul(o, toks[:, 1, hs[h]], vtok[:, hs[h]], start=False, stop=True)
                    mm.then_inc(*rp.did(("y1s1" if c == 0 else "y2", j)))
                pe.wait_ge(*rd.after(("ys", j)))
                pe.matmul(psum[:, 7, 0:SEQ], T["head_center"], ys, start=True, stop=True) \
                    .then_inc(*rp.did(("yc", j)))
            pe.wait_ge(*ra.after("ysq"))
            for j in range(8):
                mm = pe.matmul(psum[0:LANES, 0, 0:SEQ], T["half_to_row"][:, 14 - 2 * j:30 - 2 * j],
                               y_sq[:, j], start=j == 0, stop=j == 7)
            mm.then_inc(*rp.did("ysum"))
            pe.wait_ge(*ra.after("yr"))
            for j in range(8):
                b = j % 2
                pe.wait_ge(loaded_g2[b], 16 * (j // 2 + 1))
                if j >= 2:
                    pe.wait_ge(*rd.after(("y3", j - 2)))
                for h in range(2):
                    pe.matmul(psum[h * RHD:(h + 1) * RHD, 2 + b, 0:SEQ],
                              ident[0:LANES, 2 * j + h:2 * j + h + 1].broadcast_to([LANES, RHD]),
                              rows_kk[:, 0:SEQ], start=True, stop=True)
                pe.matmul(psum[:, 4 + b, 0:SEQ], g2s[:, b, 0:P], sg[:, 0], start=True, stop=False)
                pe.matmul(psum[:, 4 + b, 0:SEQ], g2s[:, b, P:2 * P], sg[:, 1], start=False, stop=True) \
                    .then_inc(*rp.did(("out", j)))

        kk_used = sem("kk_used")

        def rwkv_act():
            s = nc.scalar
            s.wait_ge(*rd.after(("z", 24)))
            s.wait_ge(*rd.after("ones_row"))
            s.activation(tw[0:LORA, :], z[0:LORA, 24, 1:ZP], ACT.Tanh).then_inc(*ra.did("tanh"))
            s.wait_ge(*rd.after(("z", 27)))
            s.activation(sg, z[:, 26:28, 1 + META:ZP], ACT.Sigmoid).then_inc(*ra.did("sigm"))
            for j in range(8):
                s.wait_ge(*rd.after(("z", 8 + j)))
                if j >= 2:
                    s.wait_ge(kk_used, j - 1)
                s.activation(diff[:, j % 2], zt(8 + j), ACT.Square, scale=vb(V_KK + j)) \
                    .then_inc(*ra.did(("kksq", j)))
            s.wait_ge(*rd.after("kkinv"))
            s.activation(rows_kk, rows_kk, ACT.Sqrt).then_inc(*ra.did("kkr"))
            for j in range(8):
                s.wait_ge(*rp.after(("logits", j)))
                s.activation(ld[0:META, 0], psum[0:META, 0, 0:P], ACT.Tanh, scale=0.5)
                s.activation(ld[:, 1:3], psum[:, 0, P:3 * P].rearrange("p (a b) -> p a b", a=2),
                             ACT.Tanh, scale=0.5).then_inc(*ra.did(("ld", j)))
                s.activation(a_t, psum[:, 1, 0:TOK], ACT.Tanh, scale=0.5, bias=half_a0[:, j:j + 1]) \
                    .then_inc(*ra.did(("a", j)))
                s.wait_ge(*rp.after(("sums", j)))
                s.activation(ar[:, 0], psum[:, 3, 0:TOK], ACT.Exp)
                s.activation(ar[:, 1], psum[:, 4, 0:TOK], ACT.Exp)
                s.activation(einv, psum[:, 4, 0:TOK], ACT.Exp, scale=-1.0)
                s.activation(eaux, psum[:, 5, 0:9], ACT.Exp).then_inc(*ra.did(("exp", j)))
                s.wait_ge(*rp.after(("toks", j)))
                s.activation(toks.rearrange("p a b -> p (a b)"), psum[:, 6, :], ACT.Copy)
                s.activation(tokm[0:META].rearrange("p a b -> p (a b)"), psum[0:META, 7, 0:3 * P],
                             ACT.Copy).then_inc(*ra.did(("toks", j)))
            s.wait_ge(*rd.after(("yc", 7)))
            s.activation(y_sq, z[:, 0:8, 1 + META:ZP], ACT.Square).then_inc(*ra.did("ysq"))
            s.wait_ge(*rd.after("yinv"))
            s.activation(rows_kk[:, 0:SEQ], rows_kk[:, 0:SEQ], ACT.Sqrt).then_inc(*ra.did("yr"))

        def rwkv_dve():
            v = nc.vector

            shifts = (shift, a_t, kf)

            def shift_of(q):
                n = Z_ORDER[q]
                rows = LORA if n in (24, 25) else P
                if q >= 3:
                    v.wait_ge(*rd.after(("z", Z_ORDER[q - 3])))
                v.tensor_tensor(shifts[q % 3][0:rows], z[0:rows, n, 0:TOK], z[0:rows, n, 1:ZP],
                                ALU.subtract).then_inc(*rd.did(("d", n)))

            def lerp(q):
                n = Z_ORDER[q]
                rows = LORA if n in (24, 25) else P
                mu = (MU_RKV + n) if n < 24 else (MU_W, MU_A, MU_G, MU_G + 1)[n - 24]
                v.wait_ge(*rd.after(("d", n)))
                v.scalar_tensor_tensor(out=z[0:rows, n, 1:ZP], in0=shifts[q % 3][0:rows],
                                       scalar=vec[0:rows, 1, mu:mu + 1], in1=z[0:rows, n, 1:ZP],
                                       op0=ALU.mult, op1=ALU.add).then_inc(*rd.did(("z", n)))

            v.memset(z[:, :, 0:1], 0.0).then_inc(*rd.did("zero"))
            v.memset(tw[LORA:LORA + 1, :], 1.0).then_inc(*rd.did("ones_row"))
            v.memset(gm, 0.0).then_inc(*rd.did("gm_zero"))
            v.wait_ge(*rd.after("zero"))
            v.tensor_scalar(half_a0[:, :], vec[:, 1, V_A0:V_A0 + 8], 0.5, None, ALU.mult)
            for q in range(len(Z_ORDER) + 1):
                if q < len(Z_ORDER):
                    shift_of(q)
                if q:
                    lerp(q - 1)
            v.wait_ge(*rp.after("kksum"))
            v.tensor_scalar(rows_kk, psum[0:LANES, 0, 0:TOK], 1e-24, None, ALU.max) \
                .then_inc(*rd.did("kkvar"))
            v.wait_ge(*rd.after("kkvar"))
            v.reciprocal(rows_kk, rows_kk).then_inc(*rd.did("kkinv"))
            for j in range(8):
                R_, K_, V_ = zt(j), zt(8 + j), zt(16 + j)
                D_ = lambda n: rd.did((n, j))
                A_ = lambda n: rd.after((n, j))
                v.wait_ge(*ra.after(("ld", j)))
                v.tensor_scalar(ld[0:META, 0], ld[0:META, 0], 0.5, 0.5, ALU.mult, ALU.add)
                v.tensor_scalar(ld[:, 1:3], ld[:, 1:3], 0.5, 0.5, ALU.mult, ALU.add).then_inc(*D_("ld"))
                v.wait_ge(*ra.after(("a", j)))
                v.tensor_scalar(a_t, a_t, 0.5, 0.5, ALU.mult, ALU.add).then_inc(*D_("a"))
                v.wait_ge(*A_("a"))
                v.tensor_scalar(kf, a_t, 1.0, vb(V_KA + j), ALU.subtract, ALU.mult).then_inc(*D_("t1"))
                v.wait_ge(*A_("t1"))
                v.scalar_tensor_tensor(out=kf, in0=kf, scalar=1.0, in1=K_, op0=ALU.add, op1=ALU.mult) \
                    .then_inc(*D_("kf"))
                v.wait_ge(*rp.after(("kkspread", j)))
                v.scalar_tensor_tensor(out=kkn, in0=K_, scalar=vb(V_KK + j), in1=psum[:, 2, 0:TOK],
                                       op0=ALU.mult, op1=ALU.mult).then_inc(*D_("kkn"))
                v.wait_ge(*A_("kf"))
                v.scalar_tensor_tensor(out=diff[:, 0], in0=R_, scalar=vb(V_RK + j), in1=kf,
                                       op0=ALU.mult, op1=ALU.mult).then_inc(*D_("rk"))
                v.wait_ge(*A_("kkn"))
                v.tensor_tensor(bh, kkn, a_t, ALU.mult).then_inc(*D_("b"))
                v.wait_ge(*A_("b"))
                v.wait_ge(*ra.after(("exp", j)))
                v.tensor_tensor(bh, bh, einv, ALU.mult).then_inc(*D_("bh"))
                v.tensor_tensor(kh, kf, einv, ALU.mult).then_inc(*D_("kh"))
                v.scalar_tensor_tensor(out=ar[:, 0], in0=kkn, scalar=-1.0, in1=ar[:, 0], op0=ALU.mult,
                                       op1=ALU.mult).then_inc(*D_("ah"))
                v.tensor_tensor(ar[:, 1], R_, ar[:, 1], ALU.mult).then_inc(*D_("rh"))
                v.wait_ge(*rp.after(("toks", j)))
                v.tensor_tensor(V_, psum[:, 0, 0:TOK], V_, ALU.mult).then_inc(*D_("bv"))
                v.wait_ge(*rp.after(("gram", j)))
                v.wait_ge(*rd.after("gm_zero"))
                mask = T["gram_mask"]
                v.tensor_tensor(gm[0:64].rearrange("p q (g c) -> p (q g) c", g=2),
                                psum[0:64, 0:4, :].rearrange("p q (g c) -> p (q g) c", g=2),
                                mask[0:64].unsqueeze(1).broadcast_to([64, 8, 2 * P]), ALU.mult)
                v.tensor_tensor(gm[64:P].rearrange("p q (g a t) -> p (q g) a t", g=2, a=2)[:, :, :, 64:P],
                                psum[64:P, 0:4, :].rearrange("p q (g a t) -> p (q g) a t", g=2, a=2)[:, :, :, 64:P],
                                mask[64:P].rearrange("p (a t) -> p a t", a=2)[:, :, 64:P].unsqueeze(1)
                                .broadcast_to([64, 8, 2, 64]), ALU.mult).then_inc(*D_("gram"))
                v.tensor_tensor(gm0[0:META].rearrange("p h (n t) -> p h n t", n=2),
                                psum[0:META, 4:6, 0:2 * META].rearrange("p h (n t) -> p h n t", n=2),
                                mask[0:META, 0:META].unsqueeze(1).unsqueeze(1)
                                .broadcast_to([META, 2, 2, META]), ALU.mult).then_inc(*D_("gram0"))

                PEA = lambda n: rp.after((n, j))

                def both_sizes(h, meta=True):
                    hc = slice(2 * h, 2 * h + 2)
                    yield (lambda n: inv_s[n][:, hc],
                           lambda bank: psum[:, 2 * h + bank, 0:2 * P].rearrange("p (q t) -> p q t", q=2),
                           gm[:, hc, 0:P], lambda t: t.unsqueeze(1).broadcast_to([P, 2, P]))
                    if meta:
                        yield (lambda n: inv_m[n][0:META, h],
                               lambda bank: psum[0:META, 2 * h + bank, 2 * P:2 * P + META],
                               gm0[0:META, h, 0:META], lambda t: t[0:META, 0:META])

                def step(name, h, f, wait_for=None, meta=True):
                    if wait_for:
                        v.wait_ge(*wait_for)
                    for args in both_sizes(h, meta):
                        ins = f(*args)
                    ins.then_inc(*D_((name, h)))

                TTn, copy, heads = v.tensor_tensor, v.tensor_copy, range(2)
                v.wait_ge(*A_("gram0"))
                for h in heads:
                    step("n8", h, lambda s, p, n, t: TTn(s(2), n, t(T["upper8"]), ALU.mult))
                for h in heads:
                    step("nt8", h, lambda s, p, n, t: TTn(s(0), p(0), t(T["lower8"]), ALU.mult),
                         PEA(("nt", h)))
                for h in heads:
                    step("int8", h, lambda s, p, n, t: TTn(s(1), s(0), t(ident), ALU.add),
                         A_(("nt8", h)))
                for h in heads:
                    step("p2", h, lambda s, p, n, t: copy(s(3), p(0)), PEA(("p2", h)))
                    step("ip2", h, lambda s, p, n, t: TTn(s(5), p(0), t(ident), ALU.add))
                    step("p2t", h, lambda s, p, n, t: copy(s(4), p(1)))
                for h in heads:
                    step("ip4", h, lambda s, p, n, t: TTn(s(3), p(0), t(ident), ALU.add),
                         PEA(("p4", h)))
                    step("r1t", h, lambda s, p, n, t: copy(s(4), p(1)))
                for h in heads:
                    step("nm16", h, lambda s, p, n, t: TTn(s(2), n, t(T["join16"]), ALU.mult))
                for h in heads:
                    step("r", h, lambda s, p, n, t: copy(s(0), p(0)), PEA(("r", h)))
                    step("rt", h, lambda s, p, n, t: copy(s(1), p(1)))
                for m in (16, 32, 64):
                    for h in heads:
                        step(f"p{m}", h, lambda s, p, n, t: copy(s(3), p(0)), PEA((f"p{m}", h)), m == 16)
                    if m < 64:
                        for h in heads:
                            step(f"nm{2 * m}", h, lambda s, p, n, t: TTn(
                                s(2), n, t(T[f"join{2 * m}"]), ALU.mult), meta=False)
                    for h in heads:
                        v.wait_ge(*A_(("rt" if m == 16 else f"rt{m // 2}", h)))
                        step(f"r{m}", h, lambda s, p, n, t: TTn(s(0), p(0), s(0), ALU.add),
                             PEA((f"d{m}", h)), m == 16)
                        step(f"rt{m}", h, lambda s, p, n, t: TTn(s(1), p(1), s(1), ALU.add),
                             meta=m == 16)
                for h in heads:
                    v.wait_ge(*PEA(("p128", h)))
                    copy(inv_s[3][64:P, 2 * h:2 * h + 2, 0:64],
                         psum[64:P, 2 * h, 0:2 * P].rearrange("p (q t) -> p q t", q=2)[:, :, 0:64]) \
                        .then_inc(*D_(("p128", h)))
                for h in heads:
                    v.wait_ge(*PEA(("d128", h)))
                    copy(inv_s[0][0:64, 2 * h:2 * h + 2, 64:P],
                         psum[0:64, 2 * h + 1, 0:2 * P].rearrange("p (q t) -> p q t", q=2)[:, :, 0:64]) \
                        .then_inc(*D_(("r128", h)))
                v.wait_ge(*PEA("x0"))
                v.tensor_copy(xs[0:META], psum[0:META, 0, 0:P].rearrange("p (h v) -> p h v", h=2)) \
                    .then_inc(*D_("x0"))
                v.wait_ge(*PEA("u0"))
                v.tensor_copy(us[0:META], psum[0:META, 1, 0:P].rearrange("p (h v) -> p h v", h=2)) \
                    .then_inc(*D_("u0"))
                v.wait_ge(*PEA("s0"))
                v.tensor_scalar(state, psum[:, 2, 0:RHD], eaux[:, 1:2], None, ALU.mult) \
                    .then_inc(*D_("s0"))
                v.wait_ge(*A_("s0"))
                v.tensor_scalar(state_h, state, eaux[:, 3:4], None, ALU.mult).then_inc(*D_("sh1"))
                for c in (1, 2):
                    v.wait_ge(*PEA(f"x{c}"))
                    v.tensor_copy(xs, psum[:, 0:2, 0:RHD]).then_inc(*D_(f"x{c}"))
                    v.wait_ge(*PEA(f"u{c}"))
                    v.tensor_copy(us, psum[:, 3, 0:P].rearrange("p (h v) -> p h v", h=2)) \
                        .then_inc(*D_(f"u{c}"))
                    if c == 1:
                        v.tensor_scalar(state, state, eaux[:, 5:6], None, ALU.mult).then_inc(*D_("sd"))
                        v.wait_ge(*PEA("y1s1"))
                        v.wait_ge(*A_("sd"))
                        v.scalar_tensor_tensor(out=state, in0=psum[:, 6, 0:RHD], scalar=eaux[:, 4:5],
                                               in1=state, op0=ALU.mult, op1=ALU.add) \
                            .then_inc(*D_("s1"))
                        v.wait_ge(*A_("s1"))
                        v.tensor_scalar(state_h, state, eaux[:, 6:7], None, ALU.mult) \
                            .then_inc(*D_("sh2"))
                v.wait_ge(*PEA("y2"))
                v.tensor_copy(ys.rearrange("p (c t) -> p c t", c=2), psum[:, 4:6, 0:P]) \
                    .then_inc(*D_("ys"))
                v.wait_ge(*PEA("yc"))
                v.tensor_copy(zt(j)[:, META:TOK], psum[:, 7, 0:SEQ]).then_inc(*D_("yc"))
            v.wait_ge(*rp.after("ysum"))
            rows_y = rows_kk[:, 0:SEQ]
            v.tensor_scalar(rows_y, psum[0:LANES, 0, 0:SEQ], 1.0 / RHD, GN_EPS, ALU.mult, ALU.add) \
                .then_inc(*rd.did("yvar"))
            v.wait_ge(*rd.after("yvar"))
            v.reciprocal(rows_y, rows_y).then_inc(*rd.did("yinv"))
            for j in range(8):
                yj = zt(j)[:, META:TOK]
                v.wait_ge(*rp.after(("out", j)))
                v.scalar_tensor_tensor(out=yj, in0=yj, scalar=vb(V_GNW + j), in1=psum[:, 2 + j % 2, 0:SEQ],
                                       op0=ALU.mult, op1=ALU.mult).then_inc(*rd.did(("y1", j)))
                v.wait_ge(*rd.after(("y1", j)))
                v.scalar_tensor_tensor(out=yj, in0=yj, scalar=vb(V_GNB + j), in1=zt(16 + j)[:, META:TOK],
                                       op0=ALU.add, op1=ALU.add).then_inc(*rd.did(("y2", j)))
                v.wait_ge(*rd.after(("y2", j)))
                v.tensor_tensor(yj, psum[:, 4 + j % 2, 0:SEQ], yj, ALU.mult).then_inc(*rd.did(("y3", j)))

        F0 = 8 * ZP
        fq, fk, fv = area(F0, 8, TOK), area(F0 + 8 * TOK, 8, TOK), area(F0 + 16 * TOK, 8, TOK)
        fox_all = area(F0, 24, TOK)
        at0 = F0 + 24 * TOK
        fsq = place(2, 8, TOK)
        qn, kn = place(SEQ), place(TOK)
        vt, vtm = place(2, P), place(P)
        fs_s = [place(2, META + P + TOK) for _ in range(2)]
        fwt, fwm = place(2, 384), place(2, SEQ)
        fl, fl2, fl3 = place(TOK), place(TOK), place(TOK)
        lft = place(3, LANES)
        c_neg = place(TOK)
        c_tok = place(2, LANES)
        fmx_s, fsum_s, frs_s = place(2, 4), place(2, 4), place(2, 4)
        assert at0 <= ARENA
        N1, N2 = META + P, TOK
        fr = slice(32, 32 + LANES)
        fd_steps = ["f1", "f2", "fmin", "fabs", "flog", "lft", "cneg", "ctok", "qkvar", "qkinv", "gq"]
        fa_steps = ["fexp", "fln", "qsq", "ksq", "qkr"]
        fp_steps = ["lft", "ctok", "qksum"]
        for j in range(9):
            fd_steps += [(n, j) for n in ("qn", "kn") if j < 8] + [(n, j - 1) for n in ("rs", "w") if j]
            fd_steps += [(n, j) for n in ("s10", "s20", "s11", "s21", "max1", "max2", "neg") if j < 8]
            fa_steps += [(n, j - 1) for n in ("v", "wt", "o") if j] + [("exp", j)] * (j < 8)
            fp_steps += [("spread", j)] * (j < 8) + [("v", j - 1)] * (j > 0) + [("scores", j)] * (j < 8)
            fp_steps += [(n, j - 1) for n in ("wt", "o") if j]
        fd, fa, fp = (Order(sem(n), s) for n, s in (("fox_dve", fd_steps), ("fox_act", fa_steps),
                                                    ("fox_pe", fp_steps)))
        rows_qk = small2[0:LANES]

        def fox_dve_f():
            v = nc.vector
            v.tensor_tensor(flk[fr], psum[fr, 4, 0:TOK], rstd[fr, :], ALU.mult).then_inc(*fd.did("f1"))
            v.wait_ge(fox_bias_loaded, 16)
            v.wait_ge(*fd.after("f1"))
            v.tensor_scalar(flk[fr], flk[fr], f_bias[fr, 0:1], None, ALU.add).then_inc(*fd.did("f2"))

        def fox_dve():
            v = nc.vector
            v.wait_ge(*fd.after("f2"))
            v.tensor_scalar(fl3[fr], flk[fr], 0.0, None, ALU.min).then_inc(*fd.did("fmin"))
            v.wait_ge(*fd.after("fmin"))
            v.scalar_tensor_tensor(out=fl2[fr], in0=fl3[fr], scalar=-2.0, in1=flk[fr], op0=ALU.mult,
                                   op1=ALU.add).then_inc(*fd.did("fabs"))
            v.wait_ge(*fa.after("fln"))
            v.tensor_tensor(fl3[fr], fl3[fr], fl2[fr], ALU.subtract).then_inc(*fd.did("flog"))
            v.wait_ge(*fp.after("lft"))
            v.tensor_copy(lft[0:META, 0:1], psum[0:META, 5, 0:LANES].unsqueeze(1))
            v.tensor_copy(lft[:, 1:3], psum[:, 5, LANES:3 * LANES].rearrange("p (a b) -> p a b", a=2)) \
                .then_inc(*fd.did("lft"))
            v.wait_ge(*fp.after("ctok"))
            v.tensor_scalar(c_neg[0:LANES], psum[0:LANES, 6, 0:TOK], -1.0, None, ALU.mult) \
                .then_inc(*fd.did("cneg"))
            v.tensor_copy(c_tok, psum[:, 7, 0:2 * LANES].rearrange("p (a b) -> p a b", a=2)) \
                .then_inc(*fd.did("ctok"))
            v.wait_ge(*fp.after("qksum"))
            v.tensor_scalar(rows_qk, psum[0:LANES, 0:2, 0:TOK], 1.0 / RHD, RMS_EPS, ALU.mult, ALU.add) \
                .then_inc(*fd.did("qkvar"))
            v.wait_ge(*fd.after("qkvar"))
            v.reciprocal(rows_qk, rows_qk).then_inc(*fd.did("qkinv"))
            v.tensor_scalar(lam[:, 6:7], vb(G_FQ), RHD ** -0.5, None, ALU.mult).then_inc(*fd.did("gq"))
            v.wait_ge(*fd.after("gq"))
            for j in range(9):
                D_ = lambda n: fd.did((n, j))
                if j < 8:
                    v.wait_ge(*fp.after(("spread", j)))
                    v.scalar_tensor_tensor(out=qn, in0=fq[:, j, X], scalar=lam[:, 6:7],
                                           in1=psum[:, 0, X], op0=ALU.mult, op1=ALU.mult) \
                        .then_inc(*D_("qn"))
                    v.scalar_tensor_tensor(out=kn, in0=fk[:, j], scalar=vb(G_FK), in1=psum[:, 1, 0:TOK],
                                           op0=ALU.mult, op1=ALU.mult).then_inc(*D_("kn"))
                if j > 0:
                    fs, fsum, frs = (t[(j - 1) % 2] for t in (fs_s, per(fsum_s), per(frs_s)))
                    v.wait_ge(*fa.after(("exp", j - 1)))
                    v.reciprocal(frs, fsum).then_inc(*fd.did(("rs", j - 1)))
                    v.wait_ge(*fd.after(("rs", j - 1)))
                    for h in range(2):
                        for b, part in enumerate((fs[:, h, 0:N1], fs[:, h, N1:])):
                            ins = v.tensor_scalar(part, part, frs[:, 2 * h + b:2 * h + b + 1], None,
                                                  ALU.mult)
                    ins.then_inc(*fd.did(("w", j - 1)))
                if j == 8:
                    continue
                fs, fmx = fs_s[j % 2], fmx_s[:, j % 2]
                v.wait_ge(*fp.after(("scores", j)))
                if j >= 2:
                    v.wait_ge(*fp.after(("wt", j - 2)))
                for h in range(2):
                    v.scalar_tensor_tensor(out=fs[:, h, 0:N1], in0=psum[:, 4 + h, 0:N1],
                                           scalar=c_tok[:, 0, 2 * j + h:2 * j + h + 1],
                                           in1=T["fox_mask"][:, P:TOK], op0=ALU.add, op1=ALU.add) \
                        .then_inc(*D_(f"s1{h}"))
                    v.scalar_tensor_tensor(out=fs[:, h, N1:], in0=psum[:, 4 + h, N1:N1 + N2],
                                           scalar=c_tok[:, 1, 2 * j + h:2 * j + h + 1],
                                           in1=T["fox_mask"], op0=ALU.add, op1=ALU.add) \
                        .then_inc(*D_(f"s2{h}"))
                v.wait_ge(*fd.after(("s21", j)))
                v.tensor_reduce(fmx[:, 0::2], fs[:, :, 0:N1], AX, ALU.max).then_inc(*D_("max1"))
                v.tensor_reduce(fmx[:, 1::2], fs[:, :, N1:], AX, ALU.max).then_inc(*D_("max2"))
                v.wait_ge(*fd.after(("max2", j)))
                v.tensor_scalar(fmx, fmx, -1.0, None, ALU.mult).then_inc(*D_("neg"))

        def per(t):
            return [t[:, 0], t[:, 1]]

        def fox_act():
            s = nc.scalar
            s.wait_ge(*fd.after("fabs"))
            s.activation(fl2[fr], fl2[fr], ACT.Exp, scale=-1.0).then_inc(*fa.did("fexp"))
            s.wait_ge(*fa.after("fexp"))
            s.activation(fl2[fr], fl2[fr], ACT.Ln, bias=1.0).then_inc(*fa.did("fln"))
            s.wait_ge(acc_free, L["fox"].t1)
            s.activation(fsq[:, 0], fq, ACT.Square).then_inc(*fa.did("qsq"))
            s.activation(fsq[:, 1], fk, ACT.Square).then_inc(*fa.did("ksq"))
            s.wait_ge(*fd.after("qkinv"))
            s.activation(rows_qk, rows_qk, ACT.Sqrt).then_inc(*fa.did("qkr"))
            for j in range(9):
                if j > 0:
                    s.wait_ge(*fp.after(("v", j - 1)))
                    s.activation(vt.rearrange("p a b -> p (a b)"), psum[:, 2, 0:2 * P], ACT.Copy)
                    s.activation(vtm[0:META], psum[0:META, 2, 2 * P:3 * P], ACT.Copy) \
                        .then_inc(*fa.did(("v", j - 1)))
                    s.wait_ge(*fp.after(("wt", j - 1)))
                    s.activation(fwt, psum[:, 6:8, 0:384], ACT.Copy)
                    s.activation(fwm[0:META], psum[0:META, 3, :].rearrange("p (h t) -> p h t", h=2),
                                 ACT.Copy).then_inc(*fa.did(("wt", j - 1)))
                    s.wait_ge(*fp.after(("o", j - 1)))
                    s.activation(fq[:, j - 1, X], psum[:, 2, 0:SEQ], ACT.Copy) \
                        .then_inc(*fa.did(("o", j - 1)))
                if j < 8:
                    fs, fmx, fsum = fs_s[j % 2], fmx_s[:, j % 2], fsum_s[:, j % 2]
                    s.wait_ge(*fd.after(("neg", j)))
                    for h in range(2):
                        for b, part in enumerate((fs[:, h, 0:N1], fs[:, h, N1:])):
                            n = 2 * h + b
                            ins = s.activation(part, part, ACT.Exp, bias=fmx[:, n:n + 1],
                                               accum_out=fsum[:, n:n + 1])
                    ins.then_inc(*fa.did(("exp", j)))

        def fox_pe():
            pe = nc.tensor
            pe.wait_ge(*fd.after("flog"))
            for n, t in enumerate(PIECES):
                rows = t.stop - t.start
                mm = pe.transpose(psum[0:rows, 5, n * LANES:(n + 1) * LANES], fl3[fr, t],
                                  ident[fr, 32:32 + LANES])
            mm.then_inc(*fp.did("lft"))
            pe.wait_ge(*fd.after("lft"))
            tri = T["gram_mask"][:, P:2 * P]
            for n, t in enumerate(PIECES):
                for b in range(n + 1):
                    rows = PIECES[b].stop - PIECES[b].start
                    rhs = tri[0:rows, 0:t.stop - t.start] if b == n else ones[0:rows, 0:t.stop - t.start]
                    mm = pe.matmul(psum[0:LANES, 6, t], lft[0:rows, b, :], rhs, start=b == 0, stop=b == n)
                    if n:
                        mm = pe.matmul(psum[:, 7, (n - 1) * LANES:n * LANES], rhs, lft[0:rows, b, :],
                                       start=b == 0, stop=b == n)
            mm.then_inc(*fp.did("ctok"))
            pe.wait_ge(*fa.after("ksq"))
            for n in range(2):
                for j in range(8):
                    mm = pe.matmul(psum[0:LANES, n, 0:TOK], T["half_to_row"][:, 14 - 2 * j:30 - 2 * j],
                                   fsq[:, n, j], start=j == 0, stop=j == 7)
            mm.then_inc(*fp.did("qksum"))
            pe.wait_ge(*fa.after("qkr"))
            for j in range(9):
                if j < 8:
                    for n in range(2):
                        for h in range(2):
                            mm = pe.matmul(psum[h * RHD:(h + 1) * RHD, n, 0:TOK],
                                           ident[0:LANES, 2 * j + h:2 * j + h + 1]
                                           .broadcast_to([LANES, RHD]),
                                           small2[0:LANES, n], start=True, stop=True)
                    mm.then_inc(*fp.did(("spread", j)))
                if j > 0:
                    if j > 1:
                        pe.wait_ge(*fa.after(("o", j - 2)))
                    for n in (1, 2):
                        pe.transpose(psum[:, 2, (n - 1) * P:n * P], fv[:, j - 1, PIECES[n]], ident)
                    pe.transpose(psum[0:META, 2, 2 * P:3 * P], fv[:, j - 1, PIECES[0]], ident) \
                        .then_inc(*fp.did(("v", j - 1)))
                if j < 8:
                    pe.wait_ge(*fd.after(("kn", j)))
                    for h in range(2):
                        r = slice(h * RHD, (h + 1) * RHD)
                        head = ident[0:LANES, 2 * j + h:2 * j + h + 1].broadcast_to([LANES, P])
                        for c, (o, n) in enumerate(((0, N1), (N1, N2))):
                            out_ = psum[:, 4 + h, o:o + n]
                            pe.matmul(out_, qn[r, c * P:(c + 1) * P], kn[r, 0:n], start=True, stop=False)
                            mm = pe.matmul(out_, head, c_neg[0:LANES, 0:n], start=False, stop=True)
                    mm.then_inc(*fp.did(("scores", j)))
                if j == 0:
                    continue
                fs = fs_s[(j - 1) % 2]
                pe.wait_ge(*fd.after(("w", j - 1)))
                for h in range(2):
                    w1, w2 = fs[:, h, 0:N1], fs[:, h, N1:]
                    pe.transpose(psum[:, 6 + h, 0:P], w1[:, META:N1], ident)
                    pe.transpose(psum[:, 6 + h, P:2 * P], w2[:, META:N1], ident)
                    pe.transpose(psum[:, 6 + h, 2 * P:3 * P], w2[:, N1:TOK], ident)
                    pe.transpose(psum[0:META, 3, 2 * h * P:(2 * h + 1) * P], w1[:, 0:META], ident)
                    mm = pe.transpose(psum[0:META, 3, (2 * h + 1) * P:(2 * h + 2) * P], w2[:, 0:META],
                                      ident)
                mm.then_inc(*fp.did(("wt", j - 1)))
                pe.wait_ge(*fa.after(("wt", j - 1)))
                for h in range(2):
                    r = slice(h * RHD, (h + 1) * RHD)
                    o = psum[r, 2, :]
                    pe.matmul(o[:, 0:SEQ], vtm[0:META, r], fwm[0:META, h], start=True, stop=False,
                              skip_group_check=True)
                    pe.matmul(o[:, 0:SEQ], vt[:, 0, r], fwt[:, h, 0:SEQ], start=False, stop=False,
                              skip_group_check=True)
                    mm = pe.matmul(o[:, P:SEQ], vt[:, 1, r], fwt[:, h, 256:384], start=False, stop=True,
                                   skip_group_check=True)
                mm.then_inc(*fp.did(("o", j - 1)))

        G0 = F0 + 8 * TOK
        gates = area(G0, KT * 2, SEQ)
        merged = area(G0 + 2 * KT * SEQ, KT, SEQ)
        gated = area(G0 + 3 * KT * SEQ, 4, SEQ)
        assert G0 + (3 * KT + 4) * SEQ <= ARENA
        gates_done, merged_done, added_done = sem("gates_done"), sem("merged_done"), sem("added_done")

        def y_src(k):
            return zt(k)[:, META:TOK] if k < 8 else fq[:, k - 8, X]

        def branch_evac(i, g):
            lin, v = L["branch"], nc.vector
            if isinstance(i, int) and i == 0 and g == 0:
                v.wait_ge(gates_done, 1)
            for m in range(4):
                wait_tile(lin, i, g, m)
                dst = merged[:, bass.ds(4 * i + m, 1), :] if g == 0 else gated[:, m:m + 1]
                v.tensor_tensor(dst, psum[:, m:m + 1, 0:SEQ], gates[:, bass.ds(KT * g + 4 * i + m, 1), :],
                                ALU.mult).then_inc(acc_free, 1)
            if g == 1:
                v.wait_ge(acc_free, lin.t0 + 8 * i + 8)
                part = merged[:, bass.ds(4 * i, 4), :]
                v.tensor_tensor(part, part, gated, ALU.add).then_inc(merged_done, 1)

        def add_evac(i, g):
            lin, v = L["w_o"], nc.vector
            for m in range(4):
                wait_tile(lin, i, g, m)
                t = res[:, bass.ds(4 * i + m, 1), X]
                v.tensor_tensor(t, psum[:, m:m + 1, 0:SEQ], t, ALU.add).then_inc(acc_free, 1)

        def down2_add():
            lin = L["down2"]
            for m in range(KT):
                s, last = m // 4, m | 1
                if last % 4 == 3:
                    nc.vector.wait_ge(unit_used, lin.u1 - 3 + s)
                else:
                    nc.vector.wait_ge(acc_done, lin.t0 // 4 * 3 + 3 * s + last % 4 + 1)
                nc.vector.tensor_tensor(res[:, m, X], down_out(m), res[:, m, X], ALU.add) \
                    .then_inc(acc_free, 1)

        def final_ready(k):
            return acc_free, L["down2"].t1
        y_out = area(0, 2, D)
        end_pe, end_cp, stored = sem("end_pe"), [sem("end_act"), sem("end_dve")], sem("stored")

        def end_pe_work():
            for n in range(8):
                b, g = divmod(n, 4)
                for j in range(4):
                    k = 4 * g + j
                    nc.tensor.wait_ge(*final_ready(k))
                    mm = nc.tensor.transpose(psum[:, n, j * P:(j + 1) * P],
                                             res[:, k, META + b * P:META + (b + 1) * P], ident)
                mm.then_inc(end_pe, 1)

        def end_copy(which):
            for n in range(which, 8, 2):
                b, g = divmod(n, 4)
                dst = y_out[:, b, g * 512:(g + 1) * 512]
                if which:
                    nc.vector.wait_ge(end_pe, n + 1)
                    nc.vector.tensor_copy(dst, psum[:, n, :]).then_inc(end_cp[1], 1)
                else:
                    nc.scalar.wait_ge(end_pe, n + 1)
                    nc.scalar.activation(dst, psum[:, n, :], ACT.Copy).then_inc(end_cp[0], 1)

        def end_sp():
            for b in range(2):
                for s in end_cp:
                    nc.sync.wait_ge(s, 2 * b + 2)
                nc.sync.dma_start(out[0, b * P:(b + 1) * P, :], y_out[:, b]).then_inc(stored, 16)
            nc.sync.wait_ge(stored, 32)

        block = ctx.enter_context(nc.Block())

        @block.sync
        def _(sp):
            start_sp()
            start_sp_late()
            stream_sp_first(L["w_in"], start_sp_lines)
            mixer_sp()
            stream_sp(L["w_out"])
            stream_sp(L["ffn"])
            down_sp(L["down"])
            stream_sp(L["rkv"])
            stream_sp(L["lora"])
            rwkv_sp()
            stream_sp(L["fox"])
            stream_sp(L["gates"])
            stream_sp(L["branch"])
            stream_sp(L["w_o"])
            stream_sp(L["ffn2"])
            down_sp(L["down2"])
            end_sp()

        @block.tensor
        def _(pe):
            start_pe_work()
            stream_pe(L["w_in"], X, both(parts_wait("w_in"),
                                         {1: [start_lines_pe], 3: [norm_mean("pre", X)]}))
            mixer_pe()
            stream_pe(L["w_out"], X, parts_wait("w_out"), ks=W_OUT_K)
            post_pe(0)
            stream_pe(L["ffn"], X, both(parts_wait("ffn"), {3: [norm_mean("fpre", X)]}))
            down_pe(L["down"], ACT_BASE["down"])
            post_pe(1)
            stream_pe(L["rkv"], ALL, both(parts_wait("rkv"), {3: [norm_mean("n1", ALL)]}))
            stream_pe(L["lora"], ALL, widths=lora_w)
            rwkv_pe()
            stream_pe(L["fox"], ALL)
            fox_pe()
            stream_pe(L["gates"], X)
            stream_pe(L["branch"], X, parts_wait("branch"), ks=[0, 4, 8, 12])
            stream_pe(L["w_o"], X, parts_wait("w_o"))
            stream_pe(L["ffn2"], X, both(parts_wait("ffn2"), {3: [norm_mean("n2", X)]}))
            down_pe(L["down2"], ACT_BASE["down2"])
            end_pe_work()

        @block.scalar
        def _(act):
            start_act_work()
            act.wait_ge(*start_dve.after("vec"))
            for k in range(KT):
                if k % 2 == 0:
                    act.wait_ge(*start_dve.after(("x", k)))
                part_hi("w_in", res[:, k, X], k, X, va(G_PRE + k))
            stream_act(L["w_in"], {1: [norm_square("pre", X)],
                                   4: [start_act_lambda, norm_rstd("pre", X)]})
            mixer_act()
            stream_act(L["w_out"])
            post_act(0, "post", L["w_out"].t0, "ffn", lambda k: va(G_FPRE + k), X)
            stream_act(L["ffn"], {1: [norm_square("fpre", X)], 4: [norm_rstd("fpre", X)]},
                       ffn_silu(L["ffn"], 0))
            down_act(L["down"], ACT_BASE["down"])
            post_act(1, "fpost", L["down"].t1 - KT, *BLOCK2_IN)
            stream_act(L["rkv"], {1: [norm_square("n1", ALL)], 4: [norm_rstd("n1", ALL)]})
            stream_act(L["lora"])
            rwkv_act()
            stream_act(L["fox"])
            fox_act()
            stream_act(L["gates"])
            act.wait_ge(acc_free, L["gates"].t1)
            for k in range(KT):
                if k == 8:
                    act.activation(gates, gates, ACT.Sigmoid).then_inc(gates_done, 1)
                part_hi("branch", y_src(k), k, X)
            stream_act(L["branch"])
            for k in range(KT):
                act.wait_ge(merged_done, k // 4 + 1)
                part_hi("w_o", merged[:, k], k, X)
            stream_act(L["w_o"])
            act.wait_ge(acc_free, L["w_o"].t1)
            for k in range(KT):
                part_hi("ffn2", res[:, k, X], k, X, vb(G_N2 + k))
            stream_act(L["ffn2"], {1: [norm_square("n2", X)], 4: [norm_rstd("n2", X)]},
                       ffn_silu(L["ffn2"], 1))
            down_act(L["down2"], ACT_BASE["down2"])
            end_copy(0)

        @block.vector
        def _(v):
            start_dve_work()
            for k in range(KT):
                part_lo("w_in", res[:, k, X], k, X, va(G_PRE + k))
            lin = L["w_in"]

            def to_proj(i, g):
                if isinstance(i, int) and i == 0:
                    v.wait_ge(rstd_done, NORM["pre"] + 1)
                    v.wait_ge(lines_out, 16)
                take_tiles(lin, i, g, lambda m: proj[:, bass.ds(4 * i + m, 1), :])
            stream_dve(lin, to_proj, {2: [norm_sum("pre", X)], 3: [start_dve_lines],
                                      4: [norm_inv("pre", X)]})
            mixer_dve()
            stream_dve(L["w_out"], lambda i, g: copy_tiles(
                L["w_out"], i, g, lambda m: f_out[:, bass.ds(4 * i + m, 1), :]))
            post_dve(0, "post", lambda k: va(G_POST + k), "ffn", lambda k: va(G_FPRE + k), X)
            evac = ffn_evac(L["ffn"], 0)

            def ffn_take(i, g):
                if isinstance(i, int) and i == 0 and g == 0:
                    v.wait_ge(rstd_done, NORM["fpre"] + 1)
                evac(i, g)
            stream_dve(L["ffn"], ffn_take, {2: [norm_sum("fpre", X)], 4: [norm_inv("fpre", X)]})
            down_dve(L["down"], ACT_BASE["down"])
            down_copy(L["down"])
            post_dve(1, "fpost", lambda k: va(G_FPOST + k), BLOCK2_IN[0], BLOCK2_IN[1], BLOCK2_IN[2])
            def to_z(first, widths=(P,) * 4):
                def evac(i, g):
                    if first == 0 and isinstance(i, int) and i == 0:
                        v.wait_ge(rstd_done, NORM["n1"] + 1)
                    take(L["lora" if first else "rkv"], i, g,
                         lambda m: z[:, bass.ds(first + 4 * i + m, 1), 1:ZP], ALL, widths)
                return evac
            stream_dve(L["rkv"], to_z(0), {2: [norm_sum("n1", ALL)], 4: [norm_inv("n1", ALL)]})
            stream_dve(L["lora"], to_z(24, lora_w))
            fox_dve_f()
            rwkv_dve()
            stream_dve(L["fox"], lambda i, g: take(
                L["fox"], i, g, lambda m: fox_all[:, bass.ds(4 * i + m, 1), :], ALL))
            fox_dve()
            stream_dve(L["gates"], lambda i, g: take_tiles(
                L["gates"], i, g, lambda m: gates[:, bass.ds(4 * i + m, 1), :]))
            for k in range(KT):
                part_lo("branch", y_src(k), k, X)
            stream_dve(L["branch"], branch_evac)
            for k in range(KT):
                part_lo("w_o", merged[:, k], k, X)
            stream_dve(L["w_o"], add_evac)
            for k in range(KT):
                part_lo("ffn2", res[:, k, X], k, X, vb(G_N2 + k))
            evac2 = ffn_evac(L["ffn2"], 1)

            def ffn2_take(i, g):
                if isinstance(i, int) and i == 0 and g == 0:
                    v.wait_ge(rstd_done, NORM["n2"] + 1)
                evac2(i, g)
            stream_dve(L["ffn2"], ffn2_take, {2: [norm_sum("n2", X)], 4: [norm_inv("n2", X)]})
            down_dve(L["down2"], ACT_BASE["down2"])
            down2_add()
            end_copy(1)

        @block.gpsimd
        def _(pool):
            mixer_pool()
            post_pool(0)
            post_pool(1)


_TABLES, _AT = constants()
_INS = ["x", "w_in", "w_out", "lambda_q1", "lambda_k1", "lambda_q2", "lambda_k2", "subln_gain",
        "conv_w", "conv_norm_gain", "rel_bias", "w_gate", "w_up", "w_down", "norm_mix_pre",
        "norm_mix_post", "norm_ffn_pre", "norm_ffn_post", "meta_tokens_2", "norm1_g_2", "w_in_2",
        "rwkv_mu_2", "rwkv_w0_2", "rwkv_w2_2", "rwkv_a0_2", "rwkv_a2_2", "rwkv_g2_2", "rwkv_k_k_2",
        "rwkv_k_a_2", "rwkv_r_k_2", "rwkv_gn_w_2", "rwkv_gn_b_2", "fox_q_norm_g_2", "fox_k_norm_g_2",
        "fox_f_bias_2", "w_branch_a_2", "w_branch_b_2", "w_o_2", "norm2_g_2", "w_gate_up_2",
        "w_down_2"]


def kernel(**inputs):
    import numpy as _np
    import concourse.bacc as _bacc
    from concourse import mybir as _mybir
    from concourse.bass_utils import run_bass_kernel_spmd as _run

    nc = _bacc.Bacc("TRN2", target_bir_lowering=False, num_devices=1)
    n_tab = max(e for n, (b, e) in _AT.items() if n not in ("bucket_hot", "line_mask"))
    arrays = {name: _np.ascontiguousarray(inputs[name]) for name in _INS}
    arrays["tables"] = _np.ascontiguousarray(_TABLES[:, :n_tab])
    arrays["line_tables"] = _np.ascontiguousarray(_TABLES[:, n_tab:])
    a = {name: nc.dram_tensor(name, v.shape, _mybir.dt.from_np(v.dtype), kind="ExternalInput").ap()
         for name, v in arrays.items()}
    out = nc.dram_tensor("out", (1, SEQ, D), _mybir.dt.float32, kind="ExternalOutput").ap()
    transformer_pair_kernel(nc, a, out, _AT)
    return _run(nc, [arrays], core_ids=[0]).results[0]["out"]
```
